# Optimizing a Trainium2 kernel written in Bass

```python
import math
import jax, jax.numpy as jnp
from jax import lax
import numpy as np

D_MODEL = 1024
BATCH = 1
SEQ = 512
DEPTH = 2

N_MIXERS = 2
CONV_EXPAND = 2
CONV_WIDTH = D_MODEL * CONV_EXPAND
CONV_K = 3
HEAD_DIM = 64
HEADS_PER_GROUP = D_MODEL // HEAD_DIM
DILATED_GROUPS = ((128, 1), (512, 4), (2048, 16))
N_GROUPS = len(DILATED_GROUPS)
ATTN_WIDTH = HEADS_PER_GROUP * HEAD_DIM
QKV_COLS = N_GROUPS * 3 * ATTN_WIDTH
BLOCK = 128
N_BUCKETS = 32
MAX_DISTANCE = 2048
EPS = 1e-6
N_CONV_LAYERS = (DEPTH + 1) // 2
N_ATTN_LAYERS = DEPTH // 2


def rms_norm(x, g):
    xf = x.astype(jnp.float32)
    y = xf * lax.rsqrt(jnp.mean(xf * xf, axis=-1, keepdims=True) + EPS)
    return (y * g.astype(jnp.float32)).astype(x.dtype)

def t5_bucket(dist):
    max_exact = N_BUCKETS // 2
    d = jnp.maximum(dist, 1).astype(jnp.float32)
    large = max_exact + (jnp.log(d / max_exact) / math.log(MAX_DISTANCE / max_exact)
                         * (N_BUCKETS - max_exact)).astype(jnp.int32)
    large = jnp.minimum(large, N_BUCKETS - 1)
    return jnp.where(dist < max_exact, dist, large)

def short_conv_mixer(h, w_in, w_conv, w_out):
    S = h.shape[1]
    proj = h @ w_in
    b_gate, c_gate, u, z = jnp.split(proj, 4, axis=-1)
    v = c_gate * u
    vp = jnp.pad(v, ((0, 0), (CONV_K - 1, 0), (0, 0)))
    conv = sum(w_conv[k] * vp[:, k:k + S] for k in range(CONV_K))
    y = b_gate * conv * jax.nn.silu(z)
    return y @ w_out

def dilated_group_attention(q, k, v, bias_tab, window, dilation):
    B, S, H, Dh = q.shape
    L = S // dilation
    nb = -(-L // BLOCK)
    Lp = nb * BLOCK
    span = window // dilation

    def to_sub(t):
        t = t.reshape(B, L, dilation, H, Dh).transpose(0, 2, 3, 1, 4)
        t = jnp.pad(t, ((0, 0), (0, 0), (0, 0), (0, Lp - L), (0, 0)))
        return t.reshape(B, dilation, H, nb, BLOCK, Dh)

    def band(t):
        prev = jnp.pad(t, ((0, 0), (0, 0), (0, 0), (1, 0), (0, 0), (0, 0)))[:, :, :, :-1]
        return jnp.concatenate([prev, t], axis=4)

    qs = to_sub(q)
    kb = band(to_sub(k))
    vb = band(to_sub(v))
    logits = jnp.einsum('brhnqd,brhnkd->brhnqk', qs, kb).astype(jnp.float32) * (HEAD_DIM ** -0.5)

    a = jnp.arange(BLOCK)[:, None]
    kk = jnp.arange(2 * BLOCK)[None, :]
    step = BLOCK + a - kk
    blk = jnp.arange(nb)[:, None, None]
    key_pos = (blk - 1) * BLOCK + kk[None]
    valid = (step >= 0) & (step <= span) & (key_pos >= 0)
    bucket = t5_bucket(jnp.clip(step, 0, span) * dilation)
    bias = bias_tab.astype(jnp.float32)[bucket].transpose(2, 0, 1)[:, None]

    logits = jnp.where(valid, logits + bias, -jnp.inf)
    lse = jax.nn.logsumexp(logits, axis=-1)
    probs = jnp.exp(logits - lse[..., None])
    out = jnp.einsum('brhnqk,brhnkd->brhnqd', probs.astype(v.dtype), vb)

    out = out.reshape(B, dilation, H, Lp, Dh)[:, :, :, :L]
    out = out.transpose(0, 3, 1, 2, 4).reshape(B, S, H, Dh)
    lse = lse.reshape(B, dilation, H, Lp)[:, :, :, :L]
    lse = lse.transpose(0, 3, 1, 2).reshape(B, S, H)
    return out, lse

def dilated_attention_mixer(h, w_in, q_gain, k_gain, w_out, rel_bias):
    B, S, _ = h.shape
    proj = h @ w_in
    qkv = proj[..., :QKV_COLS].reshape(B, S, N_GROUPS, 3, HEADS_PER_GROUP, HEAD_DIM)
    z = proj[..., QKV_COLS:]
    outs, lses = [], []
    for g, (window, dilation) in enumerate(DILATED_GROUPS):
        q = rms_norm(qkv[:, :, g, 0], q_gain[g])
        k = rms_norm(qkv[:, :, g, 1], k_gain[g])
        bias_g = rel_bias[:, g * HEADS_PER_GROUP:(g + 1) * HEADS_PER_GROUP]
        o, l = dilated_group_attention(q, k, qkv[:, :, g, 2], bias_g, window, dilation)
        outs.append(o)
        lses.append(l)
    alpha = jax.nn.softmax(jnp.stack(lses, axis=0), axis=0)
    o = jnp.sum(alpha[..., None] * jnp.stack(outs, axis=0).astype(jnp.float32), axis=0)
    y = o.reshape(B, S, ATTN_WIDTH).astype(h.dtype) * jax.nn.silu(z)
    return y @ w_out

def first_inputs(seed: int = 0) -> dict:
    key = jax.random.key(seed)
    ks = jax.random.split(key, 12)
    f32 = jnp.float32
    nc, na = N_CONV_LAYERS, N_ATTN_LAYERS
    x = jax.random.normal(ks[0], (BATCH, SEQ, D_MODEL), f32)
    conv_norm = 1.0 + 0.1 * jax.random.normal(ks[1], (nc, D_MODEL), f32)
    conv_w_in = jax.random.normal(ks[2], (nc, D_MODEL, 4 * CONV_WIDTH), f32) * D_MODEL ** -0.5
    conv_w = jax.random.normal(ks[3], (nc, CONV_K, CONV_WIDTH), f32) * CONV_K ** -0.5
    conv_w_out = jax.random.normal(ks[4], (nc, CONV_WIDTH, D_MODEL), f32) * CONV_WIDTH ** -0.5
    attn_norm = 1.0 + 0.1 * jax.random.normal(ks[5], (na, D_MODEL), f32)
    attn_w_in = jax.random.normal(ks[6], (na, D_MODEL, QKV_COLS + ATTN_WIDTH), f32) * D_MODEL ** -0.5
    attn_q_gain = 1.0 + 0.1 * jax.random.normal(ks[7], (na, N_GROUPS, HEAD_DIM), f32)
    attn_k_gain = 1.0 + 0.1 * jax.random.normal(ks[8], (na, N_GROUPS, HEAD_DIM), f32)
    attn_w_out = jax.random.normal(ks[9], (na, ATTN_WIDTH, D_MODEL), f32) * ATTN_WIDTH ** -0.5
    rel_bias = 0.5 * jax.random.normal(ks[10], (N_BUCKETS, N_GROUPS * HEADS_PER_GROUP), f32)
    return {"x": x, "conv_norm": conv_norm, "conv_w_in": conv_w_in, "conv_w": conv_w,
            "conv_w_out": conv_w_out, "attn_norm": attn_norm, "attn_w_in": attn_w_in,
            "attn_q_gain": attn_q_gain, "attn_k_gain": attn_k_gain, "attn_w_out": attn_w_out,
            "rel_bias": rel_bias}

def first_block(x, conv_norm, conv_w_in, conv_w, conv_w_out, attn_norm, attn_w_in,
              attn_q_gain, attn_k_gain, attn_w_out, rel_bias):
    for i in range(DEPTH):
        j = i // N_MIXERS
        if i % N_MIXERS == 0:
            h = rms_norm(x, conv_norm[j])
            x = x + short_conv_mixer(h, conv_w_in[j], conv_w[j], conv_w_out[j])
        else:
            h = rms_norm(x, attn_norm[j])
            x = x + dilated_attention_mixer(h, attn_w_in[j], attn_q_gain[j], attn_k_gain[j],
                                            attn_w_out[j], rel_bias)
    return x


D_INNER = 2 * D_MODEL
D_MLSTM = D_INNER // 2
D_RET = D_INNER - D_MLSTM
N_HEADS_MLSTM = 4
N_HEADS_RET = 4
HD_M = D_MLSTM // N_HEADS_MLSTM
HD_R = D_RET // N_HEADS_RET
CONV_K_2 = 4
CHUNK = 64
ROPE_BASE = 10000.0
D_IN_PROJ = 5 * D_MLSTM + 2 * N_HEADS_MLSTM + 4 * D_RET


def rmsnorm(x, g):
    xf = x.astype(jnp.float32)
    y = xf * lax.rsqrt(jnp.mean(xf * xf, axis=-1, keepdims=True) + EPS)
    return (y * g.astype(jnp.float32)).astype(x.dtype)

def head_layernorm(h, g, n_heads):
    B, S, W = h.shape
    hf = h.astype(jnp.float32).reshape(B, S, n_heads, W // n_heads)
    mu = jnp.mean(hf, axis=-1, keepdims=True)
    var = jnp.mean(jnp.square(hf - mu), axis=-1, keepdims=True)
    y = ((hf - mu) * lax.rsqrt(var + EPS)).reshape(B, S, W)
    return (y * g.astype(jnp.float32)).astype(h.dtype)

def causal_dwconv(x, w, b):
    S = x.shape[1]
    xp = jnp.pad(x, ((0, 0), (CONV_K_2 - 1, 0), (0, 0)))
    y = xp[:, 0:S] * w[0]
    for t in range(1, CONV_K_2):
        y = y + xp[:, t:t + S] * w[t]
    return y + b

def split_cols(p):
    sizes = [D_MLSTM] * 5 + [N_HEADS_MLSTM] * 2 + [D_RET] * 4
    idx = np.cumsum(sizes)[:-1].tolist()
    return jnp.split(p, idx, axis=-1)

def to_chunks(t):
    B, S, H, d = t.shape
    return t.reshape(B, S // CHUNK, CHUNK, H, d).transpose(1, 0, 3, 2, 4)

def from_chunks(t):
    NC, B, H, L, d = t.shape
    return t.transpose(1, 0, 3, 2, 4).reshape(B, NC * L, H * d)

def gate_chunks(t):
    B, S, H = t.shape
    return t.reshape(B, S // CHUNK, CHUNK, H).transpose(1, 0, 3, 2)

def rotary(t, positions):
    d = t.shape[-1]
    inv_freq = 1.0 / (ROPE_BASE ** jnp.linspace(0.0, 1.0, d // 2, dtype=jnp.float32))
    ang = positions.astype(jnp.float32)[..., None] * inv_freq
    cos = jnp.cos(ang)[:, :, None, :].astype(t.dtype)
    sin = jnp.sin(ang)[:, :, None, :].astype(t.dtype)
    t1, t2 = jnp.split(t, 2, axis=-1)
    return jnp.concatenate([t1 * cos - t2 * sin, t2 * cos + t1 * sin], axis=-1)

def mlstm_chunkwise(q, k, v, i_pre, f_pre):
    B, S, H, d = q.shape
    k = k * (d ** -0.5)
    li = gate_chunks(i_pre.astype(jnp.float32))
    lf = gate_chunks(jax.nn.log_sigmoid(f_pre.astype(jnp.float32)))
    causal = jnp.tril(jnp.ones((CHUNK, CHUNK), dtype=bool))

    def step(carry, inp):
        C, n, m = carry
        qj, kj, vj, lij, lfj = inp
        b = jnp.cumsum(lfj, axis=-1)
        a = b + m[..., None]
        g = b[..., :, None] - b[..., None, :] + lij[..., None, :]
        g = jnp.where(causal, g, -jnp.inf)
        m_row = jnp.maximum(a, jnp.max(g, axis=-1))
        w_intra = jnp.exp(g - m_row[..., None])
        w_inter = jnp.exp(a - m_row)
        s = jnp.einsum('bhld,bhsd->bhls', qj, kj) * w_intra
        num = (jnp.einsum('bhls,bhsv->bhlv', s, vj)
               + w_inter[..., None] * jnp.einsum('bhvk,bhlk->bhlv', C, qj))
        den = jnp.sum(s, axis=-1) + w_inter * jnp.einsum('bhk,bhlk->bhl', n, qj)
        h = num / jnp.maximum(jnp.abs(den), jnp.exp(-m_row))[..., None]
        bL = b[..., -1]
        g_end = bL[..., None] - b + lij
        m_new = jnp.maximum(bL + m, jnp.max(g_end, axis=-1))
        w_end = jnp.exp(g_end - m_new[..., None])
        decay = jnp.exp(bL + m - m_new)
        C_new = decay[..., None, None] * C + jnp.einsum('bhs,bhsv,bhsk->bhvk', w_end, vj, kj)
        n_new = decay[..., None] * n + jnp.einsum('bhs,bhsk->bhk', w_end, kj)
        return (C_new, n_new, m_new), h.astype(q.dtype)

    init = (jnp.zeros((B, H, d, d), jnp.float32),
            jnp.zeros((B, H, d), jnp.float32),
            jnp.zeros((B, H), jnp.float32))
    _, hs = lax.scan(step, init, (to_chunks(q), to_chunks(k), to_chunks(v), li, lf))
    return from_chunks(hs)

def retention_chunkwise(q, k, v):
    B, S, H, d = q.shape
    k = k * (d ** -0.5)
    log_gamma = jnp.log(1.0 - 2.0 ** (-5.0 - jnp.arange(H, dtype=jnp.float32)))
    pos = jnp.arange(CHUNK, dtype=jnp.float32)
    diff = pos[:, None] - pos[None, :]
    Dmat = jnp.where(diff >= 0, jnp.exp(log_gamma[:, None, None] * jnp.maximum(diff, 0.0)), 0.0)
    xi = jnp.exp(log_gamma[:, None] * (pos + 1.0))
    zeta = jnp.exp(log_gamma[:, None] * (CHUNK - 1.0 - pos))
    g_chunk = jnp.exp(log_gamma * CHUNK)

    def step(R, inp):
        qj, kj, vj = inp
        s = jnp.einsum('bhld,bhsd->bhls', qj, kj) * Dmat
        o = (jnp.einsum('bhls,bhsv->bhlv', s, vj)
             + xi[..., None] * jnp.einsum('bhlk,bhkv->bhlv', qj, R))
        R_new = g_chunk[:, None, None] * R + jnp.einsum('bhsk,bhsv->bhkv', kj * zeta[..., None], vj)
        return R_new, o.astype(q.dtype)

    init = jnp.zeros((B, H, d, d), jnp.float32)
    _, os_ = lax.scan(step, init, (to_chunks(q), to_chunks(k), to_chunks(v)))
    return from_chunks(os_)

def second_inputs(seed: int = 0) -> dict:
    key = jax.random.key(seed)
    ks = jax.random.split(key, 16)
    f32 = jnp.float32
    x = jax.random.normal(ks[0], (BATCH, SEQ, D_MODEL), f32)
    c = jax.random.normal(ks[1], (BATCH, D_MODEL), f32)
    offset = jax.random.randint(ks[2], (BATCH, 1), 0, 4096, dtype=jnp.int32)
    positions = offset + jnp.arange(SEQ, dtype=jnp.int32)[None, :]
    w_ada = jax.random.normal(ks[3], (DEPTH, D_MODEL, 3 * D_MODEL), f32) * (0.5 * D_MODEL ** -0.5)
    b_ada = jax.random.normal(ks[4], (DEPTH, 3 * D_MODEL), f32) * 0.02
    norm_g = 1.0 + 0.02 * jax.random.normal(ks[5], (DEPTH, D_MODEL), f32)
    w_in = jax.random.normal(ks[6], (DEPTH, D_MODEL, D_IN_PROJ), f32) * (D_MODEL ** -0.5)
    conv_w = jax.random.normal(ks[7], (DEPTH, CONV_K_2, 2 * D_MLSTM), f32) * (CONV_K_2 ** -0.5)
    conv_b = jax.random.normal(ks[8], (DEPTH, 2 * D_MLSTM), f32) * 0.02
    b_igate = jax.random.normal(ks[9], (DEPTH, N_HEADS_MLSTM), f32) * 0.1
    b_fgate = (jnp.linspace(3.0, 6.0, N_HEADS_MLSTM, dtype=f32)[None, :]
               + 0.1 * jax.random.normal(ks[10], (DEPTH, N_HEADS_MLSTM), f32))
    gn_m = 1.0 + 0.02 * jax.random.normal(ks[11], (DEPTH, D_MLSTM), f32)
    gn_r = 1.0 + 0.02 * jax.random.normal(ks[12], (DEPTH, D_RET), f32)
    w_out = jax.random.normal(ks[13], (DEPTH, D_INNER, D_MODEL), f32) * (D_INNER ** -0.5)
    final_g = 1.0 + 0.02 * jax.random.normal(ks[14], (D_MODEL,), f32)
    return {'x': x, 'c': c, 'positions': positions, 'w_ada': w_ada, 'b_ada': b_ada,
            'norm_g': norm_g, 'w_in': w_in, 'conv_w': conv_w, 'conv_b': conv_b,
            'b_igate': b_igate, 'b_fgate': b_fgate, 'gn_m': gn_m, 'gn_r': gn_r,
            'w_out': w_out, 'final_g': final_g}

def second_block(x, c, positions, w_ada, b_ada, norm_g, w_in, conv_w, conv_b,
              b_igate, b_fgate, gn_m, gn_r, w_out, final_g):
    B, S, _ = x.shape
    c_act = jax.nn.silu(c)
    for l in range(DEPTH):
        ada = c_act @ w_ada[l] + b_ada[l]
        shift, scale, gate = jnp.split(ada, 3, axis=-1)
        h = rmsnorm(x, norm_g[l]) * (1.0 + scale[:, None, :]) + shift[:, None, :]
        p = h @ w_in[l]
        mq, mk, mv, mo, mz, mi, mf, rq, rk, rv, rz = split_cols(p)

        qk = jax.nn.silu(causal_dwconv(jnp.concatenate([mq, mk], axis=-1), conv_w[l], conv_b[l]))
        mq_c, mk_c = jnp.split(qk, 2, axis=-1)
        cell = mlstm_chunkwise(mq_c.reshape(B, S, N_HEADS_MLSTM, HD_M),
                               mk_c.reshape(B, S, N_HEADS_MLSTM, HD_M),
                               mv.reshape(B, S, N_HEADS_MLSTM, HD_M),
                               mi + b_igate[l], mf + b_fgate[l])
        y_m = jax.nn.sigmoid(mo) * head_layernorm(cell, gn_m[l], N_HEADS_MLSTM) * jax.nn.silu(mz)

        rq_h = rotary(rq.reshape(B, S, N_HEADS_RET, HD_R), positions)
        rk_h = rotary(rk.reshape(B, S, N_HEADS_RET, HD_R), positions)
        ret = retention_chunkwise(rq_h, rk_h, rv.reshape(B, S, N_HEADS_RET, HD_R))
        y_r = head_layernorm(ret, gn_r[l], N_HEADS_RET) * jax.nn.silu(rz)

        y = jnp.concatenate([y_m, y_r], axis=-1) @ w_out[l]
        x = x + gate[:, None, :] * y
    return rmsnorm(x, final_g)


def setup_inputs(seed=0):
    out = dict(first_inputs(seed))
    for name, value in second_inputs(seed + 1).items():
        if name != "x":
            out[name + "_2"] = value
    return out


def reference(
    x, conv_norm, conv_w_in, conv_w, conv_w_out, attn_norm, attn_w_in, attn_q_gain, attn_k_gain,
    attn_w_out, rel_bias, c_2, positions_2, w_ada_2, b_ada_2, norm_g_2, w_in_2, conv_w_2,
    conv_b_2, b_igate_2, b_fgate_2, gn_m_2, gn_r_2, w_out_2, final_g_2,
):
    x = first_block(
        x, conv_norm, conv_w_in, conv_w, conv_w_out, attn_norm, attn_w_in, attn_q_gain,
        attn_k_gain, attn_w_out, rel_bias,
    )
    return second_block(
        x, c_2, positions_2, w_ada_2, b_ada_2, norm_g_2, w_in_2, conv_w_2, conv_b_2, b_igate_2,
        b_fgate_2, gn_m_2, gn_r_2, w_out_2, final_g_2,
    )


_drawn_inputs = setup_inputs


def setup_inputs(seed=0):
    import zlib

    import numpy as np

    out = dict(_drawn_inputs(seed))
    spreads = {}
    factors = {'attn_norm': 3.229,
     'attn_q_gain': 7.098,
     'attn_k_gain': 6.69,
     'b_ada_2': 3.049,
     'norm_g_2': 7.858,
     'conv_b_2': 64.0,
     'b_igate_2': 64.0,
     'gn_m_2': 25.0,
     'gn_r_2': 8.0,
     'final_g_2': 7.996}
    for name, (base, spread) in spreads.items():
        noise = np.random.default_rng([zlib.crc32(name.encode()), seed]).standard_normal(out[name].shape)
        drawn = base * np.exp(spread * noise) if base else spread * noise
        out[name] = __import__('jax').numpy.asarray(drawn.astype(out[name].dtype))
    for name, factor in factors.items():
        out[name] = (out[name] * factor).astype(out[name].dtype)
    return out
```

```python
from contextlib import ExitStack
import math

import numpy as np
import concourse.bass as bass
from concourse import mybir

F32 = mybir.dt.float32
F32R = mybir.dt.float32r
I32 = mybir.dt.int32
ALU = mybir.AluOpType
ACT = mybir.ActivationFunctionType
AXX = mybir.AxisListType.X
ds = bass.ds

P = 128
T = 512
D = 1024
KD = D // P
EPS = 1e-6
NEG = -1e30
PRIME = 4

E_CONV = 2 * D
KE = E_CONV // P
KC = 3
G, HD, NH = 3, 64, D // 64
HG = 4
NQUAD = NH // HG
DILATION = (1, 4, 16)
NBUCKET, MAXDIST = 32, 2048
NL = 2
CH = 4
HC = D // CH
KC2 = 4
NCELL = 2 * CH

BLK = 1024
CONV_B = 4 * KE
CONV_OUT_B = 2 * KD
ATT_B = NQUAD * (6 * G + 2)
ATT_OUT_B = KD
CELL_B = CH * (10 + 8)
GATE_B = 2
LAYER_B = GATE_B + CELL_B + 2 * KD
B_CONV_OUT = CONV_B
B_ATT = B_CONV_OUT + CONV_OUT_B
B_ATT_OUT = B_ATT + ATT_B
B_LAYER = B_ATT_OUT + ATT_OUT_B
NB = B_LAYER + NL * LAYER_B
RAW = 4
SPL = 2

C_NORM = 0
C_CONVW = C_NORM + 5 * KD
C_GAIN = C_CONVW + KC * KE
C_ADAB = C_GAIN + 2 * G
C_C = C_ADAB + NL * 3 * KD
C_FREQ = C_C + KD
NCOL = C_FREQ + 1

W0, W1 = 384, 256
NE = W0 + 2 * W1


G_ACT, G_DVE = 4, 7
ROPE_R = 7
ROUND = 1.5 * 2.0 ** 23
TWO_PI = (6.28125, 0.0019350051879882812, 3.019915981956753e-07)
PI_BELOW = 3.1415925
S_AT = ((2, 0, 0), (3, 0, T), (4, 0, T + 3 * P), (4, 2 * P, T + 5 * P))
O, ROW = 6, 7
NUM, AUX = 5, 7


def after(k):
    return k + 1 + PRIME


def program(nc, x, wstream, wada, cols, headcols, gncols, gatecols, relb, onehot, pos, ident, tri,
            decay, sel, out, upto=4):
    ctx = ExitStack()
    with ctx:
        def sb(name, shape, dt=F32, where=ctx):
            return where.enter_context(nc.sbuf_tensor(name, shape, dt))

        def sem(name):
            return ctx.enter_context(nc.semaphore(name))

        xs = sb("xs", [P, KD, T])
        h_hi = sb("h_hi", [P, KD, T], F32R)
        h_lo = sb("h_lo", [P, KD, T], F32R)
        raw = sb("raw", [P, RAW, BLK])
        w_hi = sb("w_hi", [P, SPL, BLK], F32R)
        w_lo = sb("w_lo", [P, SPL, BLK], F32R)
        colt = sb("colt", [P, NCOL])
        mods = sb("mods", [P, NL, 3 * KD])
        ones = sb("ones", [P, P])
        idt = sb("idt", [P, P])
        zcol = sb("zcol", [P, KD])
        onec = sb("onec", [P, KD])
        rstd = sb("rstd", [P, T])
        sq = sb("sq", [P, 2, T])
        psum = ctx.enter_context(nc.psum_tensor("psum", [P, 8, T], F32))
        STAT, MISC = 7, 6

        evec = nc.dram_tensor("evec", (NH, NE), F32).ap()
        toep0 = nc.dram_tensor("toep0", (NH, P, 2 * P), F32).ap()
        toep1 = nc.dram_tensor("toep1", (2, NH, P, P), F32).ap()
        qkrow = nc.dram_tensor("qkrow", (2 * HG, T), F32).ap()
        frow = nc.dram_tensor("frow", (HG, G, T), F32).ap()
        crow = nc.dram_tensor("crow", (2, CH, T), F32).ap()

        s_const = sem("s_const")
        s_xin = [sem(f"s_xin{c}") for c in range(2)]
        s_raw = [sem(f"s_raw{s}") for s in range(RAW)]
        s_out = sem("s_out")
        s_memset = sem("s_memset")
        s_go = sem("s_go")
        s_pe_go = sem("s_pe_go")
        hi_done = sem("hi_done")
        split_done = sem("split_done")
        blk_done = sem("blk_done")
        stat_mm = sem("stat_mm")
        act_evac = sem("act_evac")
        x_sq = sem("x_sq")
        norm_sd = sem("norm_sd")
        norm_rstd = sem("norm_rstd")
        h_full = sem("h_full")
        h_hi_done = sem("h_hi_done")
        h_lo_done = sem("h_lo_done")
        y_full = sem("y_full")
        y_hi_done = sem("y_hi_done")
        y_lo_done = sem("y_lo_done")
        x_upd = sem("x_upd")

        block = ctx.enter_context(nc.Block())
        OWN = {"pe": [blk_done, stat_mm], "act": [act_evac, x_sq, norm_sd, h_hi_done, y_hi_done],
               "dve": [norm_rstd, h_full, h_lo_done, y_full, y_lo_done, x_upd], "pool": []}

        def own(engine, name):
            OWN[engine].append(sem(name))
            return OWN[engine][-1]

        with ExitStack() as stage:
            y_hi = sb("y_hi", [P, KE, T], F32R, stage)
            y_lo = sb("y_lo", [P, KE, T], F32R, stage)
            hf = sb("hf", [P, 2, T], F32, stage)
            cv_c = sb("cv_c", [P, T], F32, stage)
            cv_u = sb("cv_u", [P, T], F32, stage)
            cv_z = sb("cv_z", [P, T], F32, stage)
            cv_b = sb("cv_b", [P, T], F32, stage)
            cv_v = sb("cv_v", [P, T + 2], F32, stage)
            cv_t = sb("cv_t", [P, T], F32, stage)
            adaw = sb("adaw", [P, 3 * D], F32, stage)
            adaacc = sb("adaacc", [P, 3 * D], F32, stage)
            oneh = sb("oneh", [33, NE], F32, stage)
            relt = sb("relt", [33, G * NH], F32, stage)
            esb = sb("esb", [NH, NE], F32, stage)
            cact = sb("cact", [P, KD], F32, stage)
        s_ada = sem("s_ada")
        s_evec = sem("s_evec")
        s_toep = sem("s_toep")
        cv_vd = own("dve", "cv_vd")
        cv_t0 = own("dve", "cv_t0")
        cv_t1 = own("dve", "cv_t1")
        cv_t2 = own("dve", "cv_t2")
        cv_t2b = own("dve", "cv_t2b")
        ada_raw = own("dve", "ada_raw")
        ada_zero = own("dve", "ada_zero")
        ada_mac = own("dve", "ada_mac")
        ada_out = own("dve", "ada_out")
        ada_sum = own("pe", "ada_sum")
        c_act = own("act", "c_act")
        e_mm = own("pe", "e_mm")
        e_sb = own("act", "e_sb")

        with ExitStack() as stage:
            ya_hi = sb("ya_hi", [P, KD, T], F32R, stage)
            ya_lo = sb("ya_lo", [P, KD, T], F32R, stage)
            hfa = sb("hfa", [P, 2, T], F32, stage)
            biast = sb("biast", [P, HG, 2 * P], F32, stage)
            qkraw = sb("qkraw", [P, 4, T], F32, stage)
            qkn = sb("qkn", [P, 4, T], F32, stage)
            nrmb = sb("nrmb", [P, 4, T], F32, stage)
            vt = sb("vt", [P, 4, HC], F32, stage)
            prob = sb("prob", [P, 7 * P], F32, stage)
            probT = sb("probT", [P, 7 * P], F32, stage)
            oacc = sb("oacc", [P, G, 2, T], F32, stage)
            fb = sb("fb", [P, G * T], F32, stage)
            nmc = sb("nmc", [P, 4, HG], F32, stage)
            denc = sb("denc", [P, 4, HG], F32, stage)
            nrow = sb("nrow", [HG, G, T], F32, stage)
            drow = sb("drow", [HG, G, T], F32, stage)
            mrow = sb("mrow", [HG, T], F32, stage)
            srow = sb("srow", [2 * HG, T], F32, stage)
            zs = sb("zs", [P, 2, T], F32, stage)
            yt = sb("yt", [P, T], F32, stage)
            yu = sb("yu", [P, T], F32, stage)
            selt = sb("selt", [P, 4, 2 * HG], F32, stage)
            gaint = sb("gaint", [P, 2 * G], F32, stage)
        s_sel = sem("s_sel")
        s_bias = sem("s_bias")
        s_qkw = sem("s_qkw")
        s_qkb = sem("s_qkb")
        s_fw = sem("s_fw")
        s_fb = sem("s_fb")
        gains = own("dve", "gains")
        qk_sq = own("act", "qk_sq")
        qk_stat = own("pe", "qk_stat")
        qk_sd = own("act", "qk_sd")
        qk_rstd = own("dve", "qk_rstd")
        qk_norm = own("dve", "qk_norm")
        sc_mm = own("pe", "sc_mm")
        sc_add = own("dve", "sc_add")
        sc_max = own("dve", "sc_max")
        sc_exp = own("act", "sc_exp")
        pt_mm = own("pe", "pt_mm")
        pt_cp = own("dve", "pt_cp")
        pv_mm = own("pe", "pv_mm")
        o_cp = own("dve", "o_cp")
        tr_mm = own("pe", "tr_mm")
        tr_cp = own("dve", "tr_cp")
        mg_max = own("dve", "mg_max")
        mg_exp = own("act", "mg_exp")
        mg_chain = own("dve", "mg_chain")
        mg_f = own("dve", "mg_f")
        ym_chain = own("dve", "ym_chain")

        with ExitStack() as stage:
            yl_hi = sb("yl_hi", [P, KE, T], F32R, stage)
            yl_lo = sb("yl_lo", [P, KE, T], F32R, stage)
            cosb = sb("cosb", [P, T], F32, stage)
            sinb = sb("sinb", [P, T], F32, stage)
            dect = sb("dect", [P, CH, T], F32, stage)
            trit = sb("trit", [P, P], F32, stage)
            pad = sb("pad", [P, 2, KC2 - 1 + T], F32, stage)
            tmp = sb("tmp", [P, 2, T], F32, stage)
            ql = sb("ql", [P, 2, T], F32, stage)
            kl = sb("kl", [P, 2, T], F32, stage)
            vl = sb("vl", [P, 4, HC], F32, stage)
            ol = sb("ol", [P, 2, T], F32, stage)
            zl = sb("zl", [P, 2, T], F32, stage)
            wgt = sb("wgt", [P, 10 * P], F32, stage)
            nmb = sb("nmb", [P, T], F32, stage)
            emb = sb("emb", [P, T], F32, stage)
            argd = sb("argd", [P, 4, P], F32, stage)
            hc = sb("hc", [P, 2, T], F32, stage)
            lmod = sb("lmod", [P, 3 * KD], F32, stage)
            hcol = sb("hcol", [P, 4 * (KC2 + 1)], F32, stage)
            gcol = sb("gcol", [P, 2], F32, stage)
            gbc = sb("gbc", [64, 1], F32, stage)
            ccol = sb("ccol", [P, 4, CH], F32, stage)
            cch = sb("cch", [P, 4], F32, stage)
            g_i, g_f = wgt[0:CH, 0:T], wgt[0:CH, T:2 * T]
            g_b, g_m = argd[0:CH].rearrange("p a b -> p (a b)"), nmb[0:CH, :]
            g_c, g_max = hc[0:CH, 0, :], hc[0:CH, 1, :]
        s_rope = sem("s_rope")
        s_lc = sem("s_lc")
        s_hcol = sem("s_hcol")
        s_gcol = sem("s_gcol")
        s_crw = sem("s_crw")
        s_crb = sem("s_crb")
        s_gbc = sem("s_gbc")
        rope_v = own("dve", "rope_v")
        rope_a = own("act", "rope_a")
        pad_set = own("dve", "pad_set")
        l_mod = own("dve", "l_mod")
        g_act = own("act", "g_act")
        g_dve = own("dve", "g_dve")
        cc_mm = own("pe", "cc_mm")
        cc_cp = own("dve", "cc_cp")
        cvl = own("dve", "cvl")
        cvl_t = own("dve", "cvl_t")
        qk_silu = own("act", "qk_silu")
        rot_t = own("dve", "rot_t")
        rot_d = own("dve", "rot_d")
        w_arg = own("dve", "w_arg")
        w_exp = own("act", "w_exp")
        st_mm = own("pe", "st_mm")
        a_done = own("dve", "a_done")
        nv_mm = own("pe", "nv_mm")
        den_abs = own("act", "den_abs")
        den_max = own("dve", "den_max")
        den_rec = own("dve", "den_rec")
        hc_done = own("dve", "hc_done")
        mean_mm = own("pe", "mean_mm")
        cen = own("dve", "cen")
        c_sq = own("act", "c_sq")
        var_mm = own("pe", "var_mm")
        c_sd = own("act", "c_sd")
        c_rstd = own("dve", "c_rstd")
        n_gain = own("dve", "n_gain")
        n_o = own("dve", "n_o")

        V_ATT = CONV_B
        V_LAYER = V_ATT + ATT_B
        V_PER = CELL_B + GATE_B
        Y_ATT = KE
        Y_LAYER = Y_ATT + KD

        def for_layers(eng, layer):
            if upto == 3:
                layer(0)
            else:
                with eng.Fori(0, NL) as l:
                    layer(l)

        @block.sync
        def _(sp):
            def const(dst, src, s=s_const):
                sp.dma_start(dst, src).then_inc(s, 16)

            for c in range(2):
                sp.dma_start(xs[:, 4 * c:4 * c + 4, :],
                             x[4 * c:4 * c + 4].rearrange("c p t -> p c t")).then_inc(s_xin[c], 16)
            const(colt[:], cols)
            const(relt[0:NBUCKET, :], relb)
            const(oneh[:], onehot)
            const(idt[:], ident)

            def load(n, s):
                sp.dma_start(raw[:, s, :], wstream[ds(n, 1)].rearrange("a p n -> (a p) n"))\
                  .then_inc(s_raw[s], 16)

            for s in range(RAW):
                load(s, s)
            n_blocks = (NB, B_ATT, B_LAYER, B_LAYER + LAYER_B, NB)[upto]
            n_blocks = -(-n_blocks // RAW) * RAW
            with sp.Fori(1, n_blocks // RAW) as i:
                for s in range(RAW):
                    sp.wait_ge(split_done, RAW * i + s - RAW + 1)
                    load(RAW * i + s, s)
            if upto < 4:
                s_i = upto - 1
                for oc in range(KD):
                    sp.wait_ge(x_upd, after(s_i * KD + oc))
                    sp.dma_start(out[oc], xs[:, oc, :]).then_inc(s_out, 16)
            else:
                for oc in range(KD):
                    sp.wait_ge(h_full, after(4 * KD + oc))
                    sp.dma_start(out[oc], xs[:, oc, :]).then_inc(s_out, 16)
            sp.wait_ge(s_out, 16 * KD)

        @block.gpsimd
        def _(pool):
            for i, (dst, value) in enumerate(((ones[:], 1.0), (zcol[:], 0.0), (onec[:], 1.0),
                                              (relt[NBUCKET:NBUCKET + 1, :], 1.0), (cv_v[:, 0:2], 0.0))):
                if i:
                    pool.wait_ge(s_memset, i)
                pool.memset(dst, value).then_inc(s_memset, 1)

            def split(n, s, free):
                t = s % SPL
                pool.wait_ge(s_raw[s], 16 * (n // RAW + 1) if isinstance(n, int) else free[1])
                if free[0] is not None:
                    pool.wait_ge(blk_done, free[0])
                pool.sem_inc(s_go, 1)
                pool.tensor_scalar(w_hi[:, t, :], raw[:, s, :], 1.0, 0.0, ALU.mult, ALU.add)\
                    .then_inc(hi_done, 1)
                pool.wait_ge(hi_done, n + 1)
                pool.tensor_tensor(w_lo[:, t, :], raw[:, s, :], w_hi[:, t, :].bitcast(F32), ALU.subtract)\
                    .then_inc(split_done, 1)

            for s in range(RAW):
                split(s, s, (after(s - SPL) if s >= SPL else None, None))
            n_blocks = (NB, B_ATT, B_LAYER, B_LAYER + LAYER_B, NB)[upto]
            n_blocks = -(-n_blocks // RAW) * RAW
            with pool.Fori(1, n_blocks // RAW) as i:
                for s in range(RAW):
                    split(RAW * i + s, s, (after(RAW * i + s - SPL), 16 * i + 16))

        @block.tensor
        def _(pe):
            for s in OWN["pe"]:
                pe.sem_inc(s, PRIME)

            def multiply(n, s, dst, rhs_hi, rhs_lo, k0, start, stop, rhs_ready=None):
                pe.wait_ge(split_done, n + 1)
                for k in range(KD):
                    if rhs_ready is not None:
                        pe.wait_ge(h_lo_done, rhs_ready + k)
                    hi = w_hi[:, s, k * P:(k + 1) * P]
                    lo = w_lo[:, s, k * P:(k + 1) * P]
                    pe.matmul(dst, hi, rhs_hi[:, k0 + k, :], start=start and k == 0, stop=False)
                    pe.matmul(dst, hi, rhs_lo[:, k0 + k, :], start=False, stop=False)
                    mm = pe.matmul(dst, lo, rhs_hi[:, k0 + k, :], start=False, stop=stop and k == KD - 1)
                mm.then_inc(blk_done, 1)

            def values(n, half, bank, tokens):
                pe.wait_ge(split_done, n + 1)
                for j in range(4):
                    dst = psum[:, bank + j // 2, (j % 2) * HC:(j % 2 + 1) * HC]
                    for k in range(4):
                        kk = 4 * half + k
                        first, last = kk == 0, kk == KD - 1
                        hi = w_hi[:, half, k * HC:(k + 1) * HC]
                        lo = w_lo[:, half, k * HC:(k + 1) * HC]
                        pe.matmul(dst, h_hi[:, kk, tokens(j)], hi, start=first and j % 2 == 0, stop=False,
                                  skip_group_check=True)
                        pe.matmul(dst, h_hi[:, kk, tokens(j)], lo, start=False, stop=False,
                                  skip_group_check=True)
                        mm = pe.matmul(dst, h_lo[:, kk, tokens(j)], hi, start=False,
                                       stop=last and j % 2 == 1, skip_group_check=True)
                mm.then_inc(blk_done, 1)

            def stat(i, first, last, parity):
                pe.wait_ge(x_sq, after(i))
                pe.matmul(psum[:, STAT, :], ones[:], sq[:, parity, :], start=first, stop=last)\
                    .then_inc(stat_mm, 1)

            def project_out(n0, x0, tiles, hi, lo, y_first, y_second, evacs, loop=True):
                pe.wait_ge(act_evac, after(evacs))
                pe.wait_ge(y_lo_done, after(y_first))

                def tile(i2, j, stat_before):
                    oc = 2 * i2 + j
                    pe.wait_ge(x_upd, after(x0 + oc - 2))
                    if tiles == 2 * KD:
                        multiply(n0 + 2 * oc, 0, psum[:, j, :], hi, lo, 0, True, False)
                        if stat_before:
                            stat(x0 + KD + oc - 1, False, False, 1 - j)
                        elif j == 1:
                            stat(x0 + KD + oc - 1, True, False, 1 - j)
                        pe.wait_ge(y_lo_done, after(y_second))
                        multiply(n0 + 2 * oc + 1, 1, psum[:, j, :], hi, lo, KD, False, True)
                    else:
                        multiply(n0 + oc, j, psum[:, j, :], hi, lo, 0, True, True)
                        if stat_before:
                            stat(x0 + KD + oc - 1, False, False, 1 - j)
                        elif j == 1:
                            stat(x0 + KD + oc - 1, True, False, 1 - j)

                tile(0, 0, False)
                tile(0, 1, False)
                with pe.Fori(1, KD // 2) as i2:
                    tile(i2, 0, True)
                    tile(i2, 1, True)
                stat(x0 + KD + KD - 1, False, True, 1)

            pe.wait_ge(s_memset, 5)
            for c in range(KD):
                stat(c, c == 0, c == KD - 1, c % 2)

            pe.wait_ge(s_const, 16 * 4)
            at = 0
            for g in range(G):
                width = W0 if g == 0 else W1
                pe.matmul(psum[0:NH, 4 + g, 0:width], relt[:, g * NH:(g + 1) * NH], oneh[:, at:at + width],
                          start=True, stop=True).then_inc(e_mm, 1)
                at += width

            for half in range(2):
                with pe.Fori(half * KE // 2, (half + 1) * KE // 2) as e:
                    for j in range(4):
                        pe.wait_ge(act_evac, after(4 * e + j - 4))
                        multiply(4 * e + j, j % SPL, psum[:, j, :], h_hi, h_lo, 0, True, True,
                                 after(0) if j == 0 else None)
                pe.wait_ge(ada_mac, after(half * KD + KD - 1))
                pe.wait_ge(ada_out, after(half - 1))
                if half == 0:
                    pe.wait_ge(e_sb, after(G - 1))
                for c in range(3 * KD):
                    mm = pe.matmul(psum[:, MISC, c:c + 1], adaacc[:, c * P:(c + 1) * P], ones[:, 0:1],
                                   start=True, stop=True)
                mm.then_inc(ada_sum, 1)
            project_out(B_CONV_OUT, 0, KE, y_hi, y_lo, KD - 1, KE - 1, CONV_B - 3)
            if upto == 1:
                return


            def scores(u, g, h):
                c, base = h // 2, HD * (h % 2)
                q = qkn[base:base + HD, c, :]
                k = qkn[base:base + HD, 2 + c, :]
                pe.wait_ge(qk_norm, after(4 * u + 2 * c + 1))
                pe.wait_ge(sc_add, after(4 * u + h - 1))
                if g == 0:
                    pe.matmul(psum[:, 2, 0:P], q[:, 0:P], k[:, 0:P], start=True, stop=True)
                    pe.matmul(psum[:, 2, P:3 * P], q[:, P:2 * P], k[:, 0:2 * P], start=True, stop=True)
                    pe.matmul(psum[:, 3, 0:2 * P], q[:, 2 * P:3 * P], k[:, P:3 * P], start=True, stop=True)
                    mm = pe.matmul(psum[:, 3, 2 * P:4 * P], q[:, 3 * P:], k[:, 2 * P:], start=True, stop=True)
                else:
                    for r in range(4):
                        mm = pe.matmul(psum[:, 2, r * P:(r + 1) * P], q[:, r::4], k[:, r::4],
                                       start=True, stop=True)
                mm.then_inc(sc_mm, 1)

            def turn(u, g, h):
                pe.wait_ge(sc_exp, after(4 * u + h))
                pe.wait_ge(pt_cp, after(4 * u + h - 1))
                if h == 0:
                    pe.wait_ge(tr_cp, after(2 * u - 1))
                for t in range(7 if g == 0 else 4):
                    mm = pe.transpose(psum[:, 4 + t // 4, (t % 4) * P:(t % 4 + 1) * P],
                                      prob[:, t * P:(t + 1) * P], idt[:])
                mm.then_inc(pt_mm, 1)

            def weigh(u, g, h, v_evac):
                pe.wait_ge(pt_cp, after(4 * u + h))
                if h == 0:
                    pe.wait_ge(act_evac, after(v_evac))
                pe.wait_ge(o_cp, after(2 * u + h // 2 - 1))
                base = HD * (h % 2)
                for b in range(4):
                    dst = psum[base:base + HD, O, b * P:(b + 1) * P]
                    v = vt[:, b, h * HD:(h + 1) * HD]
                    if g == 0 and b > 0:
                        before = vt[:, b - 1, h * HD:(h + 1) * HD]
                        pe.matmul(dst, before, probT[:, (2 * b - 1) * P:2 * b * P], start=True, stop=False)
                        mm = pe.matmul(dst, v, probT[:, 2 * b * P:(2 * b + 1) * P], start=False, stop=True)
                    else:
                        mm = pe.matmul(dst, v, probT[:, b * P:(b + 1) * P], start=True, stop=True)
                mm.then_inc(pv_mm, 1)

            def turn_stats(u, sd_before):
                pe.wait_ge(qk_sd, after(sd_before))
                for b in range(4):
                    mm = pe.transpose(psum[0:HG, ROW, b * P:(b + 1) * P], nmc[:, b, :], idt[:])
                mm.then_inc(tr_mm, 1)
                for b in range(4):
                    mm = pe.transpose(psum[0:HG, 4, b * P:(b + 1) * P], denc[:, b, :], idt[:])
                mm.then_inc(tr_mm, 1)

            def qk_stats(u, tr_before):
                pe.wait_ge(tr_cp, after(tr_before))
                for c in range(4):
                    pe.wait_ge(qk_sq, after(4 * u + c))
                    mm = pe.matmul(psum[0:2 * HG, ROW, :], selt[:, c, :], nrmb[:, c, :],
                                   start=(c == 0), stop=(c == 3))
                mm.then_inc(qk_stat, 1)

            def att_chunk(i, s, ready=None):
                pe.wait_ge(act_evac, after(V_ATT + i - 2))
                multiply(B_ATT + i, s, psum[:, s, :], h_hi, h_lo, 0, True, True, ready)

            def att_values(i, half, g):
                if half == 0:
                    pe.wait_ge(act_evac, after(V_ATT + i - 1))
                tokens = (lambda j: slice(j * P, (j + 1) * P)) if g == 0 else (lambda j: slice(j, T, 4))
                values(B_ATT + i + half, half, 0, tokens)

            def att_unit(quad, g):
                p, pg, i = 3 * quad + g - 1, g - 1, 20 * quad + 6 * g
                pv = V_ATT + i - 1
                att_chunk(i, 0)
                scores(p, pg, 0)
                att_chunk(i + 1, 1)
                scores(p, pg, 1)
                turn(p, pg, 0)
                att_chunk(i + 2, 0)
                scores(p, pg, 2)
                turn(p, pg, 1)
                weigh(p, pg, 0, pv)
                att_chunk(i + 3, 1)
                scores(p, pg, 3)
                turn(p, pg, 2)
                weigh(p, pg, 1, pv)
                att_values(i + 4, 0, g)
                turn(p, pg, 3)
                weigh(p, pg, 2, pv)
                qk_stats(p + 1, 2 * p - 1)
                att_values(i + 4, 1, g)
                weigh(p, pg, 3, pv)
                turn_stats(p, p + 1)

            def att_last(quad, more):
                p, i = 3 * quad + 2, 20 * quad + 18
                pv = V_ATT + i - 1
                att_chunk(i, 0)
                scores(p, 2, 0)
                att_chunk(i + 1, 1)
                scores(p, 2, 1)
                turn(p, 2, 0)
                if more:
                    att_chunk(i + 2, 0)
                scores(p, 2, 2)
                turn(p, 2, 1)
                weigh(p, 2, 0, pv)
                if more:
                    att_chunk(i + 3, 1)
                scores(p, 2, 3)
                turn(p, 2, 2)
                weigh(p, 2, 1, pv)
                if more:
                    att_chunk(i + 4, 0)
                turn(p, 2, 3)
                weigh(p, 2, 2, pv)
                if more:
                    att_chunk(i + 5, 1)
                weigh(p, 2, 3, pv)
                turn_stats(p, p)
                if more:
                    att_values(i + 6, 0, 0)
                    qk_stats(p + 1, 2 * p + 1)
                    att_values(i + 6, 1, 0)

            pe.wait_ge(s_sel, 16)
            for j in range(4):
                att_chunk(j, j % 2, after(KD) if j == 0 else None)
            att_values(4, 0, 0)
            qk_stats(0, -1)
            att_values(4, 1, 0)
            att_unit(0, 1)
            with pe.Fori(0, NQUAD - 1) as quad:
                att_unit(quad, 2)
                att_last(quad, True)
                att_unit(quad + 1, 1)
            att_unit(NQUAD - 1, 2)
            att_last(NQUAD - 1, False)
            project_out(B_ATT_OUT, KD, KD, ya_hi, ya_lo, Y_ATT + KD - 1, Y_ATT + KD - 1,
                        V_ATT + ATT_B - 1)
            if upto == 2:
                return

            def similar(U, H, mlstm):
                if mlstm:
                    pe.wait_ge(qk_silu, after(4 * H + 3))
                else:
                    pe.wait_ge(rot_d, after(4 * H + 3))
                pe.wait_ge(a_done, after(U - 1))
                for st in range(4):
                    bank, col, _ = S_AT[st]
                    width = T - st * P
                    for c in range(2):
                        mm = pe.matmul(psum[:, bank, col:col + width], kl[:, c, st * P:(st + 1) * P],
                                       ql[:, c, st * P:], start=(c == 0), stop=(c == 1))
                mm.then_inc(st_mm, 1)

            def numerator(U, mlstm):
                pe.wait_ge(a_done, after(U))
                pe.wait_ge(hc_done, after(U - 1))
                pe.wait_ge(cen, after(2 * U - 1))
                for c in range(3 if mlstm else 2):
                    for st in range(4):
                        lhs = ones[:] if c == 2 else vl[:, st, c * P:(c + 1) * P]
                        w0 = S_AT[st][2]
                        mm = pe.matmul(psum[:, NUM + c, st * P:], lhs, wgt[:, w0:w0 + T - st * P],
                                       start=(st == 0), stop=(st == 3), skip_group_check=True)
                mm.then_inc(nv_mm, 1)

            def mean(U):
                pe.wait_ge(hc_done, after(U))
                for c in range(2):
                    mm = pe.matmul(psum[:, AUX, :], ones[:], hc[:, c, :], start=(c == 0), stop=(c == 1))
                mm.then_inc(mean_mm, 1)

            def variance(U):
                pe.wait_ge(c_sq, after(2 * U + 1))
                for c in range(2):
                    mm = pe.matmul(psum[:, 2, :], ones[:], sq[:, c, :], start=(c == 0), stop=(c == 1))
                mm.then_inc(var_mm, 1)

            def layer(l):
                n0, v0, u0 = B_LAYER + LAYER_B * l, V_LAYER + V_PER * l, NCELL * l

                def chunk(i, s):
                    pe.wait_ge(act_evac, after(v0 + i - 2))
                    multiply(n0 + i, s, psum[:, s, :], h_hi, h_lo, 0, True, True)

                def cell_values(i, half):
                    if half == 0:
                        pe.wait_ge(act_evac, after(v0 + i - 1))
                    values(n0 + i + half, half, 0, lambda j: slice(j * P, (j + 1) * P))

                def unit(j, i, mlstm, before):
                    U = u0 + j - 1
                    if before:
                        similar(U, CH * l + before[0], not mlstm)
                    chunk(i, 0)
                    if before:
                        numerator(U, not mlstm)
                    chunk(i + 1, 1)
                    chunk(i + 2, 0)
                    if before:
                        mean(U)
                    chunk(i + 3, 1)
                    if not before:
                        pe.wait_ge(g_dve, after(G_DVE * l + 3))
                        pe.sem_inc(s_pe_go, 1)
                        for b in range(4):
                            mm = pe.transpose(psum[:, AUX, b * CH:(b + 1) * CH],
                                              g_c[:, b * P:(b + 1) * P], idt[0:CH, 0:CH])
                        mm.then_inc(cc_mm, 1)
                    cell_values(i + 4, 0)
                    if before:
                        variance(U)
                    cell_values(i + 4, 1)
                    for m in range(4 if mlstm else 2):
                        chunk(i + 6 + m, m % 2)

                pe.wait_ge(act_evac, after(v0 - 1))
                for b in range(GATE_B):
                    pe.wait_ge(split_done, n0 + b + 1)
                    for k in range(4):
                        kk = 4 * b + k
                        pe.wait_ge(h_lo_done, after(KD * (2 + l) + kk))
                        hi = w_hi[:, b, k * P:(k + 1) * P]
                        lo = w_lo[:, b, k * P:(k + 1) * P]
                        pe.matmul(psum[:, 1, :], hi, h_hi[:, kk, :], start=(kk == 0), stop=False)
                        pe.matmul(psum[:, 1, :], hi, h_lo[:, kk, :], start=False, stop=False)
                        mm = pe.matmul(psum[:, 1, :], lo, h_hi[:, kk, :], start=False, stop=(kk == KD - 1))
                    mm.then_inc(blk_done, 1)
                unit(0, GATE_B, True, None)
                unit(1, GATE_B + 10, False, (0,))
                with pe.Fori(1, CH) as h:
                    unit(2 * h, GATE_B + 18 * h, True, (h - 1,))
                    unit(2 * h + 1, GATE_B + 18 * h + 10, False, (h,))
                U = u0 + NCELL - 1
                similar(U, CH * l + CH - 1, False)
                numerator(U, False)
                mean(U)
                variance(U)
                project_out(n0 + GATE_B + CELL_B, KD * (2 + l), KE, yl_hi, yl_lo,
                            Y_LAYER + KE * l + KE - 3, Y_LAYER + KE * l + KE - 1, v0 + V_PER - 1)

            for_layers(pe, layer)

        @block.scalar
        def _(act):
            for s in OWN["act"]:
                act.sem_inc(s, PRIME)

            def square(i, parity):
                act.wait_ge(stat_mm, after(i - 2))
                act.activation(sq[:, parity, :], xs[:, i % KD if isinstance(i, int) else parity, :],
                               ACT.Square).then_inc(x_sq, 1)

            def norm(m, shift):
                act.wait_ge(stat_mm, after(KD * m + KD - 1))
                act.activation(rstd[:], psum[:, STAT, :], ACT.Sqrt, scale=1.0 / D, bias=EPS)\
                   .then_inc(norm_sd, 1)

            def norm_split(m, full, shift):
                for k in range(KD):
                    act.wait_ge(h_full, after(KD * m + k))
                    act.activation(h_hi[:, k, :], full[:, k % 2, :], ACT.Identity, bias=shift[:, k:k + 1])\
                       .then_inc(h_hi_done, 1)

            def squares(x0):
                for oc in range(KD):
                    act.wait_ge(x_upd, after(x0 + oc))
                    act.wait_ge(stat_mm, after(x0 + KD + oc - 2))
                    act.activation(sq[:, oc % 2, :], xs[:, oc, :], ACT.Square).then_inc(x_sq, 1)

            def evac(n, i, dst, src, func=ACT.Copy):
                act.wait_ge(blk_done, after(n))
                act.activation(dst, src, func).then_inc(act_evac, 1)

            for c in range(KD):
                act.wait_ge(s_xin[c // 4], 16)
                act.wait_ge(stat_mm, after(c - 2))
                act.activation(sq[:, c % 2, :], xs[:, c, :], ACT.Square).then_inc(x_sq, 1)
            norm(0, zcol)
            act.wait_ge(s_memset, 5)
            norm_split(0, hf, zcol)
            act.wait_ge(s_const, 16 * 4)
            act.activation(cact[:], colt[:, C_C:C_C + KD], ACT.Silu).then_inc(c_act, 1)
            at = 0
            for g in range(G):
                width = W0 if g == 0 else W1
                act.wait_ge(e_mm, after(g))
                act.activation(esb[:, at:at + width], psum[0:NH, 4 + g, 0:width], ACT.Copy).then_inc(e_sb, 1)
                at += width
            act.wait_ge(e_sb, after(G - 1))
            act.dma_start(evec, esb[:]).then_inc(s_evec, 16)
            act.wait_ge(s_evec, 16)
            act.dma_start(toep0, bass.AP(evec.tensor, P - 1, [[NE, NH], [-1, P], [1, 2 * P]]))\
               .then_inc(s_toep, 16)
            for g in range(2):
                act.dma_start(toep1[g], bass.AP(evec.tensor, W0 + g * W1 + P - 1, [[NE, NH], [-1, P], [1, P]]))\
                   .then_inc(s_toep, 16)

            with act.Fori(0, KE) as e:
                act.wait_ge(ada_mac, after(e - 1))
                act.dma_start(adaw[:], wada[ds(e, 1)].rearrange("a p n -> (a p) n")).then_inc(s_ada, 16)
                act.wait_ge(cv_vd, after(e - 1))
                evac(4 * e, 0, cv_c[:], psum[:, 0, :])
                evac(4 * e + 1, 0, cv_u[:], psum[:, 1, :])
                act.wait_ge(y_full, after(e - 1))
                evac(4 * e + 2, 0, cv_z[:], psum[:, 2, :], ACT.Silu)
                evac(4 * e + 3, 0, cv_b[:], psum[:, 3, :])
                act.wait_ge(y_full, after(e))
                act.activation(y_hi[:, ds(e, 1), :].rearrange("p a t -> p (a t)"), cv_t[:], ACT.Copy)\
                   .then_inc(y_hi_done, 1)
            squares(0)
            if upto == 1:
                return

            norm(1, zcol)
            norm_split(1, hfa, zcol)
            act.wait_ge(h_lo_done, after(2 * KD - 1))
            act.dma_start(selt[:], sel).then_inc(s_sel, 16)

            def bias_tiles(u, quad, g):
                act.wait_ge(sc_add, after(4 * u - 1))
                src = (toep0 if g == 0 else toep1[g - 1])[ds(HG * quad, HG)]
                act.dma_start(biast[:, :, 0:2 * P if g == 0 else P], src.rearrange("h p n -> p h n"))\
                   .then_inc(s_bias, 16)

            def norm_rows_out(u):
                act.wait_ge(qk_rstd, after(u))
                act.dma_start(qkrow, srow[:]).then_inc(s_qkw, 16)

            def norm_rows_in(u):
                act.wait_ge(s_qkw, 16 * u + 16)
                for half in range(2):
                    act.dma_start(nrmb[HD * half:HD * (half + 1), :, :],
                                  bass.AP(qkrow.tensor, half * T, [[0, HD], [2 * T, 4], [1, T]]))\
                       .then_inc(s_qkb, 16)

            def qk_out(u, i, c):
                act.wait_ge(qk_norm, after(4 * (u - 1) + 3))
                evac(B_ATT + i, i, qkraw[:, c, :], psum[:, c % 2, :])
                act.wait_ge(act_evac, after(V_ATT + i))
                act.activation(nrmb[:, c, :], qkraw[:, c, :], ACT.Square).then_inc(qk_sq, 1)

            def qk_root(u):
                act.wait_ge(qk_stat, after(u))
                act.activation(srow[:], psum[0:2 * HG, ROW, :], ACT.Sqrt, scale=1.0 / HD, bias=EPS)\
                   .then_inc(qk_sd, 1)

            def v_out(u, i):
                act.wait_ge(blk_done, after(B_ATT + i + 1))
                act.wait_ge(pv_mm, after(4 * (u - 1) + 3))
                for b in range(2):
                    act.activation(vt[:, 2 * b:2 * b + 2, :].rearrange("p a n -> p (a n)"), psum[:, b, :],
                                   ACT.Copy).then_inc(act_evac, 1)

            def exps(u, g, h):
                act.wait_ge(sc_max, after(4 * u + h))
                if h == 0:
                    act.wait_ge(tr_mm, after(2 * u - 1))
                at = 0
                for b in range(4):
                    width = 2 * P if g == 0 and b > 0 else P
                    e = act.activation(prob[:, at:at + width], prob[:, at:at + width], ACT.Exp,
                                       bias=nmc[:, b, h:h + 1], accum_out=denc[:, b, h:h + 1])
                    at += width
                e.then_inc(sc_exp, 1)

            def merge_rows_out(quad):
                act.wait_ge(mg_f, after(quad))
                act.dma_start(frow, nrow[:]).then_inc(s_fw, 16)

            def merge_rows_in(quad, c):
                act.wait_ge(s_fw, 16 * quad + 16)
                act.wait_ge(y_full, after(Y_ATT + 2 * quad + c - 1))
                for half in range(2):
                    act.dma_start(fb[HD * half:HD * (half + 1), :],
                                  bass.AP(frow.tensor, (2 * c + half) * G * T, [[0, HD], [1, G * T]]))\
                       .then_inc(s_fb, 16)

            def y_high(quad, c):
                act.wait_ge(y_full, after(Y_ATT + 2 * quad + c))
                act.activation(ya_hi[:, ds(2 * quad + c, 1), :].rearrange("p a t -> p (a t)"), yt[:], ACT.Copy)\
                   .then_inc(y_hi_done, 1)

            def att_unit(quad, g, merge):
                p, pg, u, i = 3 * quad + g - 1, g - 1, 3 * quad + g, 20 * quad + 6 * g
                bias_tiles(p, quad, pg)
                norm_rows_in(p)
                if merge:
                    merge_rows_out(quad - 1)
                qk_out(u, i, 0)
                exps(p, pg, 0)
                if merge:
                    merge_rows_in(quad - 1, 0)
                qk_out(u, i + 1, 1)
                exps(p, pg, 1)
                qk_out(u, i + 2, 2)
                if merge:
                    y_high(quad - 1, 0)
                    merge_rows_in(quad - 1, 1)
                exps(p, pg, 2)
                qk_out(u, i + 3, 3)
                if merge:
                    y_high(quad - 1, 1)
                exps(p, pg, 3)
                qk_root(u)
                v_out(u, i + 4)
                norm_rows_out(u)

            def att_last(quad, more):
                p, i = 3 * quad + 2, 20 * quad + 18
                bias_tiles(p, quad, 2)
                norm_rows_in(p)
                act.wait_ge(y_full, after(Y_ATT + 2 * quad - 1))
                evac(B_ATT + i, i, zs[:, 0, :], psum[:, 0, :], ACT.Silu)
                exps(p, 2, 0)
                evac(B_ATT + i + 1, i + 1, zs[:, 1, :], psum[:, 1, :], ACT.Silu)
                exps(p, 2, 1)
                if more:
                    qk_out(p + 1, i + 2, 0)
                exps(p, 2, 2)
                if more:
                    qk_out(p + 1, i + 3, 1)
                exps(p, 2, 3)
                if more:
                    qk_out(p + 1, i + 4, 2)
                    qk_out(p + 1, i + 5, 3)
                act.wait_ge(mg_max, after(quad))
                act.activation(nrow[:], nrow[:], ACT.Exp).then_inc(mg_exp, 1)
                if more:
                    qk_root(p + 1)
                    v_out(p + 1, i + 6)
                    norm_rows_out(p + 1)

            for j in range(4):
                qk_out(0, j, j)
            qk_root(0)
            v_out(0, 4)
            norm_rows_out(0)
            act.wait_ge(s_toep, 48)
            att_unit(0, 1, False)
            with act.Fori(0, NQUAD - 1) as quad:
                att_unit(quad, 2, False)
                att_last(quad, True)
                att_unit(quad + 1, 1, True)
            att_unit(NQUAD - 1, 2, False)
            att_last(NQUAD - 1, False)
            merge_rows_out(NQUAD - 1)
            for c in range(2):
                merge_rows_in(NQUAD - 1, c)
                y_high(NQUAD - 1, c)

            act.wait_ge(y_lo_done, after(Y_LAYER - 1))
            if upto > 2:
                act.dma_start(sinb[:].bitcast(I32), bass.AP(pos.tensor, 0, [[0, P], [1, T]])).then_inc(s_rope, 16)
                act.dma_start(dect[:], decay).then_inc(s_lc, 16)
                act.dma_start(trit[:], tri).then_inc(s_lc, 16)
            squares(KD)
            if upto == 2:
                return

            act.wait_ge(rope_v, after(ROPE_R))
            act.activation(sinb[:], cosb[:], ACT.Sin).then_inc(rope_a, 1)
            act.wait_ge(rope_a, after(0))
            act.activation(cosb[:], cosb[:], ACT.Sin, scale=0.5).then_inc(rope_a, 1)

            def layer(l):
                n0, v0, u0 = B_LAYER + LAYER_B * l, V_LAYER + V_PER * l, NCELL * l
                act.wait_ge(g_dve, after(G_DVE * l - 1))
                act.dma_start(gbc[:], gatecols[ds(l, 1)].rearrange("a p n -> (a p) n")).then_inc(s_gbc, 16)
                norm(2 + l, lmod)
                norm_split(2 + l, tmp, lmod)

                act.wait_ge(s_gbc, 16 * l + 16)
                act.wait_ge(blk_done, after(n0 + 1))
                act.activation(g_i, psum[0:CH, 1, :], ACT.Identity, bias=gbc[0:CH, :]).then_inc(act_evac, 1)
                act.activation(g_f, psum[32:32 + CH, 1, :], ACT.Identity, bias=gbc[32:32 + CH, :])\
                   .then_inc(act_evac, 1)
                a0 = G_ACT * l
                act.wait_ge(act_evac, after(v0 + 1))
                act.activation(g_b, g_f, ACT.Abs).then_inc(g_act, 1)
                act.wait_ge(g_act, after(a0))
                act.activation(g_b, g_b, ACT.Exp, scale=-1.0).then_inc(g_act, 1)
                act.wait_ge(g_act, after(a0 + 1))
                act.activation(g_b, g_b, ACT.Ln, bias=1.0).then_inc(g_act, 1)

                def cell_squares(U):
                    for c in range(2):
                        act.wait_ge(cen, after(2 * U + c))
                        act.activation(sq[:, c, :], hc[:, c, :], ACT.Square).then_inc(c_sq, 1)

                def cell_root(U):
                    act.wait_ge(var_mm, after(U))
                    act.activation(rstd[:], psum[:, 2, :], ACT.Sqrt, scale=1.0 / HC, bias=EPS).then_inc(c_sd, 1)

                def cell_high(U, y0, at):
                    for c in range(2):
                        act.wait_ge(y_full, after(y0 + c))
                        act.activation(yl_hi[:, ds(at + c, 1), :].rearrange("p a t -> p (a t)"), hc[:, c, :],
                                       ACT.Copy).then_inc(y_hi_done, 1)

                def gains_in(U):
                    act.wait_ge(n_gain, after(2 * U - 1))
                    act.dma_start(gcol[:], gncols[ds(U, 1)].rearrange("a p n -> (a p) n")).then_inc(s_gcol, 16)

                def v_out(i, U):
                    act.wait_ge(blk_done, after(n0 + i + 1))
                    act.wait_ge(nv_mm, after(U))
                    for b in range(2):
                        act.activation(vl[:, 2 * b:2 * b + 2, :].rearrange("p a n -> p (a n)"),
                                       psum[:, b, :], ACT.Copy).then_inc(act_evac, 1)

                def silu(H, c, U):
                    act.wait_ge(cvl, after(4 * H + c))
                    act.wait_ge(st_mm, after(U))
                    act.activation((ql if c < 2 else kl)[:, c % 2, :], tmp[:, c % 2, :], ACT.Silu)\
                       .then_inc(qk_silu, 1)

                def mlstm(h, i, before):
                    H, U, yb = CH * l + h, u0 + 2 * h, Y_LAYER + KE * l + 4 * h
                    act.wait_ge(cvl, after(4 * H - 1))
                    act.dma_start(hcol[:], headcols[ds(H, 1)].rearrange("a p n -> (a p) n")).then_inc(s_hcol, 16)
                    if before:
                        gains_in(U - 1)
                    act.wait_ge(rot_d, after(4 * H - 1))
                    evac(n0 + i, 0, pad[:, 0, KC2 - 1:], psum[:, 0, :])
                    evac(n0 + i + 1, 0, pad[:, 1, KC2 - 1:], psum[:, 1, :])
                    silu(H, 0, U - 1)
                    evac(n0 + i + 2, 0, pad[:, 0, KC2 - 1:], psum[:, 0, :])
                    silu(H, 1, U - 1)
                    evac(n0 + i + 3, 0, pad[:, 1, KC2 - 1:], psum[:, 1, :])
                    silu(H, 2, U - 1)
                    if before:
                        cell_squares(U - 1)
                    silu(H, 3, U - 1)
                    if before:
                        cell_root(U - 1)
                    v_out(i + 4, U - 1)
                    if before is False:
                        act.wait_ge(g_dve, after(G_DVE * l + G_DVE - 1))
                        act.activation(g_m, g_m, ACT.Exp, scale=-1.0).then_inc(g_act, 1)
                        act.wait_ge(g_act, after(a0 + 3))
                        act.dma_start(crow[0], g_f).then_inc(s_crw, 16)
                        act.dma_start(crow[1], g_m).then_inc(s_crw, 16)
                    evac(n0 + i + 6, 0, ol[:, 0, :], psum[:, 0, :], ACT.Sigmoid)
                    evac(n0 + i + 7, 0, ol[:, 1, :], psum[:, 1, :], ACT.Sigmoid)
                    act.wait_ge(s_crw, 32 * l + 32)
                    act.wait_ge(den_max, after(H - 1))
                    act.wait_ge(w_arg, after(H - 1))
                    for r, dst in ((0, nmb), (1, emb)):
                        act.dma_start(dst[:], crow[r][ds(h, 1), :].rearrange("a t -> (a t)").partition_broadcast(P))\
                           .then_inc(s_crb, 16)
                    if before:
                        cell_high(U - 1, yb - 2, KD + 2 * (h - 1))
                    evac(n0 + i + 8, 0, zl[:, 0, :], psum[:, 0, :], ACT.Silu)
                    evac(n0 + i + 9, 0, zl[:, 1, :], psum[:, 1, :], ACT.Silu)
                    act.wait_ge(w_arg, after(H))
                    act.wait_ge(nv_mm, after(U - 1))
                    for st in range(4):
                        w0 = S_AT[st][2]
                        e = act.activation(wgt[:, w0:w0 + P], argd[:, st, :], ACT.Exp, bias=cch[:, st:st + 1])
                        if st < 3:
                            act.activation(wgt[:, w0 + P:w0 + T - st * P], nmb[:, (st + 1) * P:], ACT.Exp,
                                           bias=cch[:, st:st + 1])
                    e.then_inc(w_exp, 1)

                def retention(h, i):
                    H, U, yb = CH * l + h, u0 + 2 * h + 1, Y_LAYER + KE * l + 4 * h + 2
                    gains_in(U - 1)
                    act.wait_ge(cvl, after(4 * H + 3))
                    evac(n0 + i, 0, pad[:, 0, KC2 - 1:], psum[:, 0, :])
                    act.wait_ge(nv_mm, after(U - 1))
                    act.activation(rstd[:], psum[:, NUM + 2, :], ACT.Abs).then_inc(den_abs, 1)
                    evac(n0 + i + 1, 0, pad[:, 1, KC2 - 1:], psum[:, 1, :])
                    act.wait_ge(rot_d, after(4 * H + 1))
                    evac(n0 + i + 2, 0, pad[:, 0, KC2 - 1:], psum[:, 0, :])
                    evac(n0 + i + 3, 0, pad[:, 1, KC2 - 1:], psum[:, 1, :])
                    cell_squares(U - 1)
                    cell_root(U - 1)
                    v_out(i + 4, U - 1)
                    act.wait_ge(y_full, after(yb - 1))
                    evac(n0 + i + 6, 0, zl[:, 0, :], psum[:, 0, :], ACT.Silu)
                    cell_high(U - 1, yb - 2, 2 * h)
                    evac(n0 + i + 7, 0, zl[:, 1, :], psum[:, 1, :], ACT.Silu)

                mlstm(0, GATE_B, False)
                retention(0, GATE_B + 10)
                with act.Fori(1, CH) as h:
                    mlstm(h, GATE_B + 18 * h, True)
                    retention(h, GATE_B + 18 * h + 10)
                U = u0 + NCELL - 1
                gains_in(U)
                cell_squares(U)
                cell_root(U)
                cell_high(U, Y_LAYER + KE * l + KE - 2, KE - 2)
                squares(KD * (2 + l))

            for_layers(act, layer)
            if upto == 4:
                norm(4, zcol)

        @block.vector
        def _(dve):
            for s in OWN["dve"]:
                dve.sem_inc(s, PRIME)

            def norm(m, full, gain, shift):
                dve.wait_ge(norm_sd, after(m))
                dve.reciprocal(rstd[:], rstd[:]).then_inc(norm_rstd, 1)
                dve.wait_ge(norm_rstd, after(m))
                for k in range(KD + 1):
                    if k < KD:
                        if k >= 2:
                            dve.wait_ge(h_lo_done, after(KD * m + k - 2))
                        dve.scalar_tensor_tensor(full[:, k % 2, :], xs[:, k, :], gain[:, k:k + 1], rstd[:],
                                                 ALU.mult, ALU.mult).then_inc(h_full, 1)
                    if k >= 1:
                        j = k - 1
                        dve.wait_ge(h_hi_done, after(KD * m + j))
                        dve.scalar_tensor_tensor(h_lo[:, j, :], full[:, j % 2, :], shift[:, j:j + 1],
                                                 h_hi[:, j, :].bitcast(F32), ALU.add, ALU.subtract)\
                           .then_inc(h_lo_done, 1)

            def update(x0, oc, gate, tiles, n0):
                dve.wait_ge(blk_done, after(n0 + (2 * oc + 1 if tiles == KE else oc)))
                dve.scalar_tensor_tensor(xs[:, oc, :], psum[:, oc % 2, :], gate[:, oc:oc + 1], xs[:, oc, :],
                                         ALU.mult, ALU.add).then_inc(x_upd, 1)

            dve.wait_ge(s_const, 16 * 4)
            dve.wait_ge(s_memset, 5)
            dve.wait_ge(s_xin[0], 16)
            dve.wait_ge(s_xin[1], 16)
            norm(0, hf, colt[:, C_NORM:C_NORM + KD], zcol)
            dve.wait_ge(c_act, after(0))

            for half in range(2):
                dve.wait_ge(ada_sum, after(half - 1))
                dve.memset(adaacc[:], 0.0).then_inc(ada_zero, 1)
                with dve.Fori(half * KE // 2, (half + 1) * KE // 2) as e:
                    dve.wait_ge(act_evac, after(4 * e + 1))
                    dve.tensor_tensor(cv_v[:, 2:], cv_c[:], cv_u[:], ALU.mult).then_inc(cv_vd, 1)
                    dve.wait_ge(cv_vd, after(e))
                    dve.wait_ge(y_hi_done, after(e - 1))
                    dve.wait_ge(y_lo_done, after(e - 1))

                    def tap(k):
                        return colt[:, ds(C_CONVW + k * KE + e, 1)]

                    dve.tensor_scalar(cv_t[:], cv_v[:, 2:], tap(2), None, ALU.mult).then_inc(cv_t0, 1)
                    dve.wait_ge(cv_t0, after(e))
                    dve.scalar_tensor_tensor(cv_t[:], cv_v[:, 1:T + 1], tap(1), cv_t[:], ALU.mult, ALU.add)\
                       .then_inc(cv_t1, 1)
                    dve.wait_ge(cv_t1, after(e))
                    dve.scalar_tensor_tensor(cv_t[:], cv_v[:, 0:T], tap(0), cv_t[:], ALU.mult, ALU.add)\
                       .then_inc(cv_t2, 1)
                    dve.wait_ge(act_evac, after(4 * e + 3))
                    dve.wait_ge(cv_t2, after(e))
                    dve.tensor_tensor(cv_b[:], cv_b[:], cv_t[:], ALU.mult).then_inc(cv_t2b, 1)
                    dve.wait_ge(cv_t2b, after(e))
                    dve.tensor_tensor(cv_t[:], cv_b[:], cv_z[:], ALU.mult).then_inc(y_full, 1)
                    dve.wait_ge(y_hi_done, after(e))
                    dve.tensor_tensor(y_lo[:, ds(e, 1), :].rearrange("p a t -> p (a t)"), cv_t[:],
                                      y_hi[:, ds(e, 1), :].rearrange("p a t -> p (a t)").bitcast(F32),
                                      ALU.subtract).then_inc(y_lo_done, 1)
                    dve.wait_ge(s_ada, 16 * e + 16)
                    dve.wait_ge(ada_mac, after(e - 1))
                    dve.wait_ge(ada_zero, after(half))
                    dve.scalar_tensor_tensor(adaacc[:], adaw[:], cact[:, ds(e - half * KD, 1)], adaacc[:],
                                             ALU.mult, ALU.add).then_inc(ada_mac, 1)
                dve.wait_ge(ada_sum, after(half))
                m = mods[:, half, :]
                b0 = C_ADAB + half * 3 * KD
                dve.tensor_tensor(m, psum[:, MISC, 0:3 * KD], colt[:, b0:b0 + 3 * KD], ALU.add)\
                   .then_inc(ada_raw, 1)
                dve.wait_ge(ada_raw, after(half))
                g0 = C_NORM + (2 + half) * KD
                dve.scalar_tensor_tensor(m[:, KD:2 * KD], m[:, KD:2 * KD], 1.0, colt[:, g0:g0 + KD],
                                         ALU.add, ALU.mult).then_inc(ada_out, 1)
            for oc in range(KD):
                update(0, oc, onec, KE, B_CONV_OUT)
            if upto == 1:
                return

            norm(1, hfa, colt[:, C_NORM + KD:C_NORM + 2 * KD], zcol)
            for g in range(G):
                c = C_GAIN + 2 * g
                dve.tensor_scalar(gaint[:, 2 * g:2 * g + 1], colt[:, c:c + 1], HD ** -0.5, None, ALU.mult)
                e = dve.tensor_copy(gaint[:, 2 * g + 1:2 * g + 2], colt[:, c + 1:c + 2])
            e.then_inc(gains, 1)
            dve.wait_ge(gains, after(0))

            def qk_normalise(u, g):
                dve.wait_ge(s_qkb, 32 * u + 32)
                dve.wait_ge(sc_mm, after(4 * (u - 1) + 3))
                for c in (0, 2, 1, 3):
                    dve.scalar_tensor_tensor(qkn[:, c, :], qkraw[:, c, :],
                                             gaint[:, 2 * g + c // 2:2 * g + c // 2 + 1], nrmb[:, c, :],
                                             ALU.mult, ALU.mult).then_inc(qk_norm, 1)

            def logits(u, g, h):
                if h == 0:
                    dve.wait_ge(s_bias, 16 * u + 16)
                    dve.wait_ge(tr_mm, after(2 * u - 2))
                dve.wait_ge(sc_mm, after(4 * u + h))
                dve.wait_ge(pt_mm, after(4 * u + h - 1))
                if g == 0:
                    dve.tensor_tensor(prob[:, 0:P], psum[:, 2, 0:P], biast[:, h, P:], ALU.add)
                    dve.tensor_tensor(prob[:, P:3 * P], psum[:, 2, P:3 * P], biast[:, h, :], ALU.add)
                    dve.tensor_tensor(prob[:, 3 * P:].rearrange("p (a n) -> p a n", a=2),
                                      psum[:, 3, :].rearrange("p (a n) -> p a n", a=2),
                                      biast[:, h:h + 1, :].broadcast_to([P, 2, 2 * P]), ALU.add)\
                       .then_inc(sc_add, 1)
                    dve.wait_ge(sc_add, after(4 * u + h))
                    dve.tensor_reduce(nmc[:, 0:1, h], prob[:, 0:P], AXX, ALU.max, negate=True)
                    dve.tensor_reduce(nmc[:, 1:4, h], prob[:, P:].rearrange("p (a n) -> p a n", a=3), AXX,
                                      ALU.max, negate=True).then_inc(sc_max, 1)
                else:
                    dve.tensor_tensor(prob[:, 0:4 * P].rearrange("p (a n) -> p a n", a=4),
                                      psum[:, 2, :].rearrange("p (a n) -> p a n", a=4),
                                      biast[:, h:h + 1, 0:P].broadcast_to([P, 4, P]), ALU.add)\
                       .then_inc(sc_add, 1)
                    dve.wait_ge(sc_add, after(4 * u + h))
                    dve.tensor_reduce(nmc[:, :, h], prob[:, 0:4 * P].rearrange("p (a n) -> p a n", a=4), AXX,
                                      ALU.max, negate=True).then_inc(sc_max, 1)

            def turned(u, g, h):
                dve.wait_ge(pt_mm, after(4 * u + h))
                dve.wait_ge(pv_mm, after(4 * u + h - 1))
                if g == 0:
                    dve.tensor_copy(probT[:, 0:4 * P], psum[:, 4, :])
                    dve.tensor_copy(probT[:, 4 * P:], psum[:, 5, 0:3 * P]).then_inc(pt_cp, 1)
                else:
                    dve.tensor_copy(probT[:, 0:4 * P], psum[:, 4, :]).then_inc(pt_cp, 1)

            def natural(ap, g):
                return ap if g == 0 else ap.rearrange("p (i r) -> p r i", r=4)

            def as_queries(ap, g):
                return ap if g == 0 else ap.rearrange("p (r i) -> p r i", r=4)

            def outputs(u, g, c):
                dve.wait_ge(pv_mm, after(4 * u + 2 * c + 1))
                dve.tensor_copy(natural(oacc[:, g, c, :], g), as_queries(psum[:, O, :], g)).then_inc(o_cp, 1)

            def stats(u, g):
                dve.wait_ge(tr_mm, after(2 * u))
                dve.tensor_copy(natural(nrow[:, g, :], g), as_queries(psum[0:HG, ROW, :], g)).then_inc(tr_cp, 1)
                dve.wait_ge(tr_mm, after(2 * u + 1))
                dve.tensor_copy(natural(drow[:, g, :], g), as_queries(psum[0:HG, 4, :], g)).then_inc(tr_cp, 1)

            def qk_reciprocal(u):
                dve.wait_ge(qk_sd, after(u))
                dve.reciprocal(srow[:], srow[:]).then_inc(qk_rstd, 1)

            def merge_max(quad):
                k = 7 * quad
                dve.wait_ge(tr_cp, after(6 * quad + 5))
                dve.tensor_tensor(mrow[:], nrow[:, 0, :], nrow[:, 1, :], ALU.min).then_inc(mg_chain, 1)
                dve.wait_ge(mg_chain, after(k))
                dve.tensor_tensor(mrow[:], mrow[:], nrow[:, 2, :], ALU.min).then_inc(mg_chain, 1)
                dve.wait_ge(mg_chain, after(k + 1))
                dve.tensor_tensor(nrow[:], mrow[:].rearrange("p (a t) -> p a t", a=1).broadcast_to([HG, G, T]),
                                  nrow[:], ALU.subtract).then_inc(mg_max, 1)

            def merge_weights(quad):
                k = 7 * quad
                dve.wait_ge(mg_exp, after(quad))
                dve.tensor_tensor(drow[:], drow[:], nrow[:], ALU.mult).then_inc(mg_chain, 1)
                dve.wait_ge(mg_chain, after(k + 2))
                dve.tensor_tensor(mrow[:], drow[:, 0, :], drow[:, 1, :], ALU.add).then_inc(mg_chain, 1)
                dve.wait_ge(mg_chain, after(k + 3))
                dve.tensor_tensor(mrow[:], mrow[:], drow[:, 2, :], ALU.add).then_inc(mg_chain, 1)
                dve.wait_ge(mg_chain, after(k + 4))
                dve.reciprocal(mrow[:], mrow[:]).then_inc(mg_chain, 1)
                dve.wait_ge(mg_chain, after(k + 5))
                dve.tensor_tensor(nrow[:], nrow[:],
                                  mrow[:].rearrange("p (a t) -> p a t", a=1).broadcast_to([HG, G, T]),
                                  ALU.mult).then_inc(mg_chain, 1)
                dve.wait_ge(mg_chain, after(k + 6))
                dve.nop().then_inc(mg_f, 1)

            def merged(quad, c):
                k = 5 * (2 * quad + c)
                y = Y_ATT + 2 * quad + c
                dve.wait_ge(s_fb, 32 * (2 * quad + c) + 32)
                dve.wait_ge(y_hi_done, after(y - 1))
                dve.wait_ge(y_lo_done, after(y - 1))
                dve.tensor_tensor(yt[:], oacc[:, 0, c, :], fb[:, 0:T], ALU.mult).then_inc(ym_chain, 1)
                for g in (1, 2):
                    dve.tensor_tensor(yu[:], oacc[:, g, c, :], fb[:, g * T:(g + 1) * T], ALU.mult)\
                       .then_inc(ym_chain, 1)
                    dve.wait_ge(ym_chain, after(k + 2 * g - 1))
                    dve.tensor_tensor(yt[:], yt[:], yu[:], ALU.add).then_inc(ym_chain, 1)
                    dve.wait_ge(ym_chain, after(k + 2 * g))
                dve.tensor_tensor(yt[:], yt[:], zs[:, c, :], ALU.mult).then_inc(y_full, 1)
                dve.wait_ge(y_hi_done, after(y))
                at = ds(2 * quad + c, 1)
                dve.tensor_tensor(ya_lo[:, at, :].rearrange("p a t -> p (a t)"), yt[:],
                                  ya_hi[:, at, :].rearrange("p a t -> p (a t)").bitcast(F32), ALU.subtract)\
                   .then_inc(y_lo_done, 1)

            def att_unit(quad, g, merge):
                p, pg, u = 3 * quad + g - 1, g - 1, 3 * quad + g
                qk_normalise(p, pg)
                logits(p, pg, 0)
                logits(p, pg, 1)
                turned(p, pg, 0)
                if merge:
                    merged(quad - 1, 0)
                logits(p, pg, 2)
                turned(p, pg, 1)
                if merge:
                    merged(quad - 1, 1)
                logits(p, pg, 3)
                turned(p, pg, 2)
                outputs(p, pg, 0)
                turned(p, pg, 3)
                qk_reciprocal(u)
                outputs(p, pg, 1)
                stats(p, pg)

            def att_last(quad, more):
                p = 3 * quad + 2
                qk_normalise(p, 2)
                logits(p, 2, 0)
                logits(p, 2, 1)
                turned(p, 2, 0)
                logits(p, 2, 2)
                turned(p, 2, 1)
                logits(p, 2, 3)
                turned(p, 2, 2)
                outputs(p, 2, 0)
                turned(p, 2, 3)
                outputs(p, 2, 1)
                stats(p, 2)
                merge_max(quad)
                if more:
                    qk_reciprocal(p + 1)
                merge_weights(quad)

            qk_reciprocal(0)
            att_unit(0, 1, False)
            with dve.Fori(0, NQUAD - 1) as quad:
                att_unit(quad, 2, False)
                att_last(quad, True)
                att_unit(quad + 1, 1, True)
            att_unit(NQUAD - 1, 2, False)
            att_last(NQUAD - 1, False)
            merged(NQUAD - 1, 0)
            merged(NQUAD - 1, 1)

            def rope(i, instruction):
                instruction.then_inc(rope_v, 1)
                dve.wait_ge(rope_v, after(i))

            update(KD, 0, onec, KD, B_ATT_OUT)
            update(KD, 1, onec, KD, B_ATT_OUT)
            if upto > 2:
                dve.wait_ge(s_rope, 16)
                rope(0, dve.tensor_copy(cosb[:], sinb[:].bitcast(I32)))
                rope(1, dve.tensor_scalar(cosb[:], cosb[:], colt[:, C_FREQ:C_FREQ + 1], None, ALU.mult))
                rope(2, dve.tensor_scalar(sinb[:], cosb[:], 1.0 / (2 * math.pi), ROUND, ALU.mult, ALU.add))
            update(KD, 2, onec, KD, B_ATT_OUT)
            update(KD, 3, onec, KD, B_ATT_OUT)
            if upto > 2:
                rope(3, dve.tensor_scalar(sinb[:], sinb[:], ROUND, None, ALU.subtract))
                rope(4, dve.scalar_tensor_tensor(cosb[:], sinb[:], -TWO_PI[0], cosb[:], ALU.mult, ALU.add))
                rope(5, dve.scalar_tensor_tensor(cosb[:], sinb[:], -TWO_PI[1], cosb[:], ALU.mult, ALU.add))
            update(KD, 4, onec, KD, B_ATT_OUT)
            update(KD, 5, onec, KD, B_ATT_OUT)
            if upto > 2:
                rope(6, dve.scalar_tensor_tensor(cosb[:], sinb[:], -TWO_PI[2], cosb[:], ALU.mult, ALU.add))
                rope(7, dve.tensor_scalar(cosb[:], cosb[:], PI_BELOW, -PI_BELOW, ALU.min, ALU.max))
                dve.memset(pad[:, :, 0:KC2 - 1], 0.0).then_inc(pad_set, 1)
            update(KD, 6, onec, KD, B_ATT_OUT)
            update(KD, 7, onec, KD, B_ATT_OUT)
            if upto == 2:
                return
            dve.wait_ge(rope_a, after(1))
            rope(8, dve.scalar_tensor_tensor(cosb[:], cosb[:], -2.0, cosb[:], ALU.mult, ALU.mult))
            rope(9, dve.tensor_scalar(cosb[:], cosb[:], 1.0, None, ALU.add))
            dve.wait_ge(s_lc, 32)

            def layer(l):
                n0, v0, u0 = B_LAYER + LAYER_B * l, V_LAYER + V_PER * l, NCELL * l
                dve.wait_ge(x_upd, after(KD * (2 + l) - 1))
                dve.tensor_copy(lmod[:], mods[:, ds(l, 1), :].rearrange("p a n -> p (a n)")).then_inc(l_mod, 1)
                dve.wait_ge(l_mod, after(l))
                norm(2 + l, tmp, lmod[:, KD:2 * KD], lmod)

                d0 = G_DVE * l

                def gate(i, instruction):
                    instruction.then_inc(g_dve, 1)
                    dve.wait_ge(g_dve, after(d0 + i))

                dve.memset(rstd[0:CH, :], 1.0)
                dve.wait_ge(g_act, after(G_ACT * l + 2))
                gate(0, dve.tensor_scalar(g_f, g_f, 0.0, None, ALU.min))
                gate(1, dve.tensor_tensor(g_f, g_f, g_b, ALU.subtract))
                gate(2, dve.tensor_tensor_scan(g_b, rstd[0:CH, :], g_f, 0.0, ALU.mult, ALU.add))
                gate(3, dve.tensor_tensor(g_c, g_i, g_b, ALU.subtract))
                gate(4, dve.tensor_tensor_scan(g_max, g_c, g_c, 0.0, ALU.max, ALU.max))
                gate(5, dve.tensor_tensor(g_m, g_b, g_max, ALU.add))
                gate(6, dve.tensor_scalar(g_f, g_max, -1.0, None, ALU.mult))
                dve.wait_ge(cc_mm, after(l))
                dve.tensor_copy(ccol[:].rearrange("p a b -> p (a b)"), psum[:, AUX, 0:4 * CH]).then_inc(cc_cp, 1)

                def centre(U):
                    for c in range(2):
                        dve.wait_ge(mean_mm, after(U))
                        dve.scalar_tensor_tensor(hc[:, c, :], psum[:, AUX, :], -1.0 / HC, hc[:, c, :], ALU.mult,
                                                 ALU.add).then_inc(cen, 1)

                def finish(U, yb, at, mlstm):
                    dve.wait_ge(c_sd, after(U))
                    dve.reciprocal(rstd[:], rstd[:]).then_inc(c_rstd, 1)
                    dve.wait_ge(c_rstd, after(U))
                    dve.wait_ge(s_gcol, 16 * U + 16)
                    for c in range(2):
                        dve.scalar_tensor_tensor(hc[:, c, :], hc[:, c, :], gcol[:, c:c + 1], rstd[:],
                                                 ALU.mult, ALU.mult).then_inc(n_gain, 1)
                    if mlstm is not None:
                        for c in range(2):
                            dve.wait_ge(n_gain, after(2 * U + c))
                            dve.tensor_tensor(hc[:, c, :], hc[:, c, :], ol[:, c, :], ALU.mult).then_inc(n_o, 1)
                    for c in range(2):
                        if mlstm is not None:
                            dve.wait_ge(n_o, after(2 * mlstm + c))
                        else:
                            dve.wait_ge(n_gain, after(2 * U + c))
                        dve.tensor_tensor(hc[:, c, :], hc[:, c, :], zl[:, c, :], ALU.mult).then_inc(y_full, 1)
                    for c in range(2):
                        dve.wait_ge(y_hi_done, after(yb + c))
                        dst = ds(at + c, 1)
                        dve.tensor_tensor(yl_lo[:, dst, :].rearrange("p a t -> p (a t)"), hc[:, c, :],
                                          yl_hi[:, dst, :].rearrange("p a t -> p (a t)").bitcast(F32),
                                          ALU.subtract).then_inc(y_lo_done, 1)

                def decayed(U, h):
                    dve.wait_ge(st_mm, after(U))
                    dve.wait_ge(nv_mm, after(U - 1))
                    for st in range(4):
                        bank, col, w0 = S_AT[st]
                        width = T - st * P
                        e = dve.tensor_tensor(wgt[:, w0:w0 + width], psum[:, bank, col:col + width],
                                              dect[:, ds(h, 1), 0:width].rearrange("p a t -> p (a t)"), ALU.mult)
                    e.then_inc(a_done, 1)

                def weighed(U, H):
                    dve.wait_ge(st_mm, after(U))
                    dve.wait_ge(w_exp, after(H))
                    for bank, w0, w1 in ((2, 0, T), (3, T, T + 3 * P), (4, T + 3 * P, 10 * P)):
                        e = dve.scalar_tensor_tensor(wgt[:, w0:w1], psum[:, bank, 0:w1 - w0], HC ** -0.5,
                                                     wgt[:, w0:w1], ALU.mult, ALU.mult)
                    e.then_inc(a_done, 1)

                def conv(H, c, n):
                    k = 3 * (4 * H + c)
                    src, dst = pad[:, c % 2, :], tmp[:, c % 2, :]
                    w = hcol[:, c * (KC2 + 1):(c + 1) * (KC2 + 1)]
                    dve.wait_ge(act_evac, after(n))
                    dve.wait_ge(qk_silu, after(4 * H + c - 2))
                    dve.tensor_scalar(dst, src[:, 3:], w[:, 3:4], w[:, 4:5], ALU.mult, ALU.add).then_inc(cvl_t, 1)
                    for j in range(2):
                        dve.wait_ge(cvl_t, after(k + j))
                        dve.scalar_tensor_tensor(dst, src[:, 2 - j:2 - j + T], w[:, 2 - j:3 - j], dst,
                                                 ALU.mult, ALU.add).then_inc(cvl_t, 1)
                    dve.wait_ge(cvl_t, after(k + 2))
                    dve.scalar_tensor_tensor(dst, src[:, 0:T], w[:, 0:1], dst, ALU.mult, ALU.add)\
                       .then_inc(cvl, 1)

                def rotate(H, i, dst, n, U):
                    a, b = pad[:, 0, KC2 - 1:], pad[:, 1, KC2 - 1:]
                    k = 6 * (2 * H + i)
                    dve.wait_ge(act_evac, after(n))
                    dve.wait_ge(st_mm, after(U))
                    dve.tensor_tensor(tmp[:, 0, :], a, cosb[:], ALU.mult).then_inc(rot_t, 1)
                    dve.tensor_tensor(tmp[:, 1, :], b, sinb[:], ALU.mult).then_inc(rot_t, 1)
                    dve.wait_ge(rot_t, after(k + 1))
                    dve.tensor_tensor(dst[:, 0, :], tmp[:, 0, :], tmp[:, 1, :], ALU.subtract).then_inc(rot_t, 1)
                    dve.wait_ge(rot_t, after(k + 2))
                    dve.tensor_tensor(tmp[:, 0, :], b, cosb[:], ALU.mult).then_inc(rot_t, 1)
                    dve.tensor_tensor(tmp[:, 1, :], a, sinb[:], ALU.mult).then_inc(rot_t, 1)
                    dve.wait_ge(rot_t, after(k + 4))
                    dve.nop().then_inc(rot_d, 1)
                    dve.tensor_tensor(dst[:, 1, :], tmp[:, 0, :], tmp[:, 1, :], ALU.add).then_inc(rot_t, 1)
                    dve.wait_ge(rot_t, after(k + 5))
                    dve.nop().then_inc(rot_d, 1)

                def mlstm(h, i, before):
                    H, U, yb = CH * l + h, u0 + 2 * h, Y_LAYER + KE * l + 4 * h
                    if before:
                        decayed(U - 1, h - 1)
                    dve.wait_ge(s_hcol, 16 * H + 16)
                    conv(H, 0, v0 + i)
                    if before:
                        dve.wait_ge(nv_mm, after(U - 1))
                        for c in range(2):
                            e = dve.tensor_copy(hc[:, c, :], psum[:, NUM + c, :])
                        e.then_inc(hc_done, 1)
                    conv(H, 1, v0 + i + 1)
                    conv(H, 2, v0 + i + 2)
                    if before:
                        centre(U - 1)
                    conv(H, 3, v0 + i + 3)
                    if before:
                        finish(U - 1, yb - 2, KD + 2 * (h - 1), None)
                    dve.wait_ge(s_crb, 32 * H + 32)
                    dve.wait_ge(w_exp, after(H - 1))
                    dve.wait_ge(cc_cp, after(l))
                    dve.tensor_copy(cch[:], ccol[:, :, ds(h, 1)].rearrange("p a b -> p (a b)"))
                    dve.tensor_tensor(argd[:], nmb[:].rearrange("p (a b) -> p a b", a=4),
                                      trit[:].rearrange("p (a b) -> p a b", a=1).broadcast_to([P, 4, P]),
                                      ALU.add).then_inc(w_arg, 1)

                def retention(h, i):
                    H, U, yb = CH * l + h, u0 + 2 * h + 1, Y_LAYER + KE * l + 4 * h + 2
                    weighed(U - 1, H)
                    dve.wait_ge(den_abs, after(H))
                    dve.tensor_tensor(rstd[:], rstd[:], emb[:], ALU.max).then_inc(den_max, 1)
                    dve.wait_ge(den_max, after(H))
                    dve.reciprocal(rstd[:], rstd[:]).then_inc(den_rec, 1)
                    dve.wait_ge(den_rec, after(H))
                    for c in range(2):
                        e = dve.tensor_tensor(hc[:, c, :], psum[:, NUM + c, :], rstd[:], ALU.mult)
                    e.then_inc(hc_done, 1)
                    rotate(H, 0, ql, v0 + i + 1, U - 1)
                    centre(U - 1)
                    rotate(H, 1, kl, v0 + i + 3, U - 1)
                    finish(U - 1, yb - 2, 2 * h, H)

                mlstm(0, GATE_B, False)
                retention(0, GATE_B + 10)
                with dve.Fori(1, CH) as h:
                    mlstm(h, GATE_B + 18 * h, True)
                    retention(h, GATE_B + 18 * h + 10)
                U = u0 + NCELL - 1
                decayed(U, CH - 1)
                dve.wait_ge(nv_mm, after(U))
                for c in range(2):
                    e = dve.tensor_copy(hc[:, c, :], psum[:, NUM + c, :])
                e.then_inc(hc_done, 1)
                centre(U)
                finish(U, Y_LAYER + KE * l + KE - 2, KE - 2, None)
                for oc in range(KD):
                    update(KD * (2 + l), oc, lmod[:, 2 * KD:], KE, n0 + GATE_B + CELL_B)

            for_layers(dve, layer)
            if upto == 4:
                dve.wait_ge(norm_sd, after(4))
                dve.reciprocal(rstd[:], rstd[:]).then_inc(norm_rstd, 1)
                dve.wait_ge(norm_rstd, after(4))
                for k in range(KD):
                    c = C_NORM + 4 * KD + k
                    dve.scalar_tensor_tensor(xs[:, k, :], xs[:, k, :], colt[:, c:c + 1], rstd[:],
                                             ALU.mult, ALU.mult).then_inc(h_full, 1)


def chunk(w, c0, k0=0):
    return w[k0 * P:(k0 + KD) * P, c0:c0 + P].reshape(KD, P, P).transpose(1, 0, 2).reshape(P, BLK)


def value_chunks(w, c0):
    return [w[b * 4 * P:(b + 1) * 4 * P, c0:c0 + HC].reshape(4, P, HC).transpose(1, 0, 2).reshape(P, BLK)
            for b in range(2)]


def out_chunks(w):
    return [chunk(w, oc * P, k0) for oc in range(KD) for k0 in range(0, w.shape[0] // P, KD)]


def weight_stream(conv_w_in, conv_w_out, attn_w_in, attn_w_out, w_in_2, w_out_2):
    blocks = [chunk(conv_w_in[0], part * E_CONV + e * P) for e in range(KE) for part in (1, 2, 3, 0)]
    blocks += out_chunks(conv_w_out[0])
    w = attn_w_in[0]
    for quad in range(NQUAD):
        for g in range(G):
            at = lambda part: (g * 3 + part) * D + quad * HG * HD
            blocks += [chunk(w, at(part) + c * P) for part in range(2) for c in range(2)]
            blocks += value_chunks(w, at(2))
        blocks += [chunk(w, 9 * D + quad * HG * HD + c * P) for c in range(2)]
    blocks += out_chunks(attn_w_out[0])
    for l in range(NL):
        w = w_in_2[l]
        gates = np.zeros((D, P), w.dtype)
        gates[:, 0:CH] = w[:, 5 * D:5 * D + CH]
        gates[:, 32:32 + CH] = w[:, 5 * D + CH:5 * D + 2 * CH]
        for b in range(GATE_B):
            half = np.zeros((P, BLK), w.dtype)
            half[:, 0:4 * P] = gates[b * 4 * P:(b + 1) * 4 * P].reshape(4, P, P).transpose(1, 0, 2).reshape(P, 4 * P)
            blocks.append(half)
        m, r = 0, 5 * D + 2 * CH
        for h in range(CH):
            for part in (0, 1):
                blocks += [chunk(w, m + part * D + h * HC + c * P) for c in range(2)]
            blocks += value_chunks(w, m + 2 * D + h * HC)
            for part in (3, 4):
                blocks += [chunk(w, m + part * D + h * HC + c * P) for c in range(2)]
            for part in (0, 1):
                blocks += [chunk(w, r + part * D + h * HC + c * P) for c in range(2)]
            blocks += value_chunks(w, r + 2 * D + h * HC)
            blocks += [chunk(w, r + 3 * D + h * HC + c * P) for c in range(2)]
        blocks += out_chunks(w_out_2[l])
    return np.stack(blocks)


def by_partition(v):
    return np.ascontiguousarray(v.reshape(-1, P).T)


def bucket(dist):
    exact = NBUCKET // 2
    d = np.maximum(dist, 1).astype(np.float32)
    large = exact + (np.log(d / exact) / math.log(MAXDIST / exact) * (NBUCKET - exact)).astype(np.int32)
    return np.where(dist < exact, dist, np.minimum(large, NBUCKET - 1))


def shape_constants():
    onehot = np.zeros((NBUCKET + 1, NE), np.float32)
    onehot[NBUCKET] = NEG
    for n in range(2 * P + P - 1):
        step = 2 * P - 1 - n
        if 0 <= step <= P:
            onehot[:, n] = 0
            onehot[bucket(np.int32(step * DILATION[0])), n] = 1
    for n in range(P):
        for g in (1, 2):
            if (P - 1 - n) % (DILATION[g] // 4) == 0:
                col = W0 + (g - 1) * W1 + n
                onehot[:, col] = 0
                onehot[bucket(np.int32(4 * (P - 1 - n))), col] = 1
    s, t = np.arange(P)[:, None], np.arange(T)[None]
    gamma = np.log(1.0 - 2.0 ** (-5.0 - np.arange(CH)))
    decay = np.where(t >= s, np.exp(gamma[:, None, None] * np.maximum(t - s, 0)) * HC ** -0.5, 0.0)
    sel = np.zeros((P, 4, 2 * HG), np.float32)
    for c in range(4):
        sel[:HD, c, 2 * c] = sel[HD:, c, 2 * c + 1] = 1
    freq = (np.float32(1) / np.float32(10000.0) ** np.linspace(0, 1, P, dtype=np.float32)).astype(np.float32)
    return {
        "onehot": onehot, "ident": np.eye(P, dtype=np.float32),
        "tri": np.where(s > t[:, :P], NEG, 0).astype(np.float32),
        "decay": np.ascontiguousarray(decay.transpose(1, 0, 2)).astype(np.float32), "sel": sel,
    }, freq[:, None]


def kernel(x, conv_norm, conv_w_in, conv_w, conv_w_out, attn_norm, attn_w_in, attn_q_gain, attn_k_gain,
           attn_w_out, rel_bias, c_2, positions_2, w_ada_2, b_ada_2, norm_g_2, w_in_2, conv_w_2, conv_b_2,
           b_igate_2, b_fgate_2, gn_m_2, gn_r_2, w_out_2, final_g_2):
    import concourse.bacc as bacc
    from concourse.bass_utils import run_bass_kernel_spmd as run

    consts, freq = shape_constants()
    gains = [np.concatenate([v[0, g], v[0, g]])[:, None] for g in range(G) for v in (attn_q_gain, attn_k_gain)]
    cols = np.concatenate(
        [by_partition(conv_norm), by_partition(attn_norm), by_partition(norm_g_2), by_partition(final_g_2),
         by_partition(conv_w), *gains, by_partition(b_ada_2), by_partition(c_2), freq], axis=1)
    taps = np.concatenate([conv_w_2, conv_b_2[:, None]], axis=1).reshape(NL, KC2 + 1, 2, CH, 2, P)
    headcols = taps.transpose(0, 3, 5, 2, 4, 1).reshape(NL * CH, P, 4 * (KC2 + 1))
    gn = np.stack([gn_m_2.reshape(NL, CH, 2, P), gn_r_2.reshape(NL, CH, 2, P)], axis=2)
    gncols = gn.transpose(0, 1, 2, 4, 3).reshape(NL * NCELL, P, 2)
    gatecols = np.zeros((NL, 64, 1), b_igate_2.dtype)
    gatecols[:, 0:CH, 0] = b_igate_2
    gatecols[:, 32:32 + CH, 0] = b_fgate_2
    arrays = {
        "x": x[0].T.reshape(KD, P, T),
        "wstream": weight_stream(conv_w_in, conv_w_out, attn_w_in, attn_w_out, w_in_2, w_out_2),
        "wada": w_ada_2.reshape(NL * KD, P, 3 * D),
        "cols": cols, "headcols": headcols, "gncols": gncols, "gatecols": gatecols, "relb": rel_bias,
        "onehot": consts["onehot"], "pos": positions_2.reshape(1, T), "ident": consts["ident"],
        "tri": consts["tri"], "decay": consts["decay"], "sel": consts["sel"],
    }
    nc = bacc.Bacc("TRN2", target_bir_lowering=False, num_devices=1)
    ins, args = {}, []
    for name, a in arrays.items():
        ins[f"in_{name}"] = a = np.ascontiguousarray(a)
        args.append(nc.dram_tensor(f"in_{name}", a.shape, mybir.dt.from_np(a.dtype), kind="ExternalInput").ap())
    args.append(nc.dram_tensor("out", (KD, P, T), F32, kind="ExternalOutput").ap())
    program(nc, *args)
    r = run(nc, [ins], core_ids=[0])
    return np.ascontiguousarray(r.results[0]["out"].reshape(D, T).T).reshape(1, T, D)
```

```python
from contextlib import ExitStack
import math

import numpy as np
import concourse.bass as bass
from concourse import mybir

F32 = mybir.dt.float32
F32R = mybir.dt.float32r
I32 = mybir.dt.int32
ALU = mybir.AluOpType
ACT = mybir.ActivationFunctionType
AXX = mybir.AxisListType.X
ds = bass.ds

P = 128
T = 512
D = 1024
KD = D // P
EPS = 1e-6
NEG = -1e30
PRIME = 4

E_CONV = 2 * D
KE = E_CONV // P
KC = 3
G, HD, NH = 3, 64, D // 64
HG = 4
NQUAD = NH // HG
DILATION = (1, 4, 16)
NBUCKET, MAXDIST = 32, 2048
NL = 2
CH = 4
HC = D // CH
KC2 = 4
NCELL = 2 * CH

BLK = 1024
CONV_B = 4 * KE
CONV_OUT_B = 2 * KD
ATT_B = NQUAD * (6 * G + 2)
ATT_OUT_B = KD
CELL_B = CH * (10 + 8)
GATE_B = 2
LAYER_B = GATE_B + CELL_B + 2 * KD
B_CONV_OUT = CONV_B
B_ATT = B_CONV_OUT + CONV_OUT_B
B_ATT_OUT = B_ATT + ATT_B
B_LAYER = B_ATT_OUT + ATT_OUT_B
NB = B_LAYER + NL * LAYER_B
RAW = 4
SPL = 2

C_NORM = 0
C_CONVW = C_NORM + 5 * KD
C_GAIN = C_CONVW + KC * KE
C_ADAB = C_GAIN + 2 * G
C_C = C_ADAB + NL * 3 * KD
C_FREQ = C_C + KD
NCOL = C_FREQ + 1

W0, W1 = 384, 256
NE = W0 + 2 * W1


G_ACT, G_DVE = 4, 7
ROPE_R = 7
ROUND = 1.5 * 2.0 ** 23
TWO_PI = (6.28125, 0.0019350051879882812, 3.019915981956753e-07)
PI_BELOW = 3.1415925
SQ_ADD = KD - 1
OUT_MM = 6
STAT, NORM, MISC = 2, 3, 6
GATE = 4
CONV_OUT = (0, 1, 2, 3, 4, 5, 7, 6)
ATT_OUT = (0, 1, 3, 5, 2, 4, 6, 7)
LAYER_OUT = (0, 1, 3, 4, 2, 5, 6, 7)
S_AT = ((2, 0, 0), (3, 0, T), (4, 0, T + 3 * P), (4, 2 * P, T + 5 * P))
S_PIECES = ((2, 0, T), (3, T, T + 3 * P), (4, T + 3 * P, 10 * P))
NP = len(S_PIECES)
O, ROW = 6, 7
NUM, AUX = 5, 7


def after(k):
    return k + 1 + PRIME


def program(nc, x, wstream, wada, cols, headcols, gncols, gatecols, relb, onehot, pos, ident, tri,
            decay, sel, out):
    ctx = ExitStack()
    with ctx:
        def sb(name, shape, dt=F32, where=ctx):
            return where.enter_context(nc.sbuf_tensor(name, shape, dt))

        def sem(name):
            return ctx.enter_context(nc.semaphore(name))

        with ExitStack() as over:
            qksq_hi = sb("qksq_hi", [P, 4, T], F32R, over)
        with ExitStack() as over:
            wgt_hi = sb("wgt_hi", [P, 10 * P], F32R, over)
        with ExitStack() as over:
            qk_lo = sb("qk_lo", [P, 4, T], F32R, over)
            v_lo = sb("v_lo", [P, 4, HC], F32R, over)
        xs = sb("xs", [P, KD, T])
        h_hi = sb("h_hi", [P, KD, T], F32R)
        h_lo = sb("h_lo", [P, KD, T], F32R)
        raw = sb("raw", [P, RAW, BLK])
        w_hi = sb("w_hi", [P, SPL, BLK], F32R)
        w_lo = sb("w_lo", [P, SPL, BLK], F32R)
        colt = sb("colt", [P, NCOL])
        mods = sb("mods", [P, NL, 3 * KD])
        ones = sb("ones", [P, P])
        idt = sb("idt", [P, P])
        zcol = sb("zcol", [P, KD])
        onec = sb("onec", [P, KD])
        rstd = sb("rstd", [P, T])
        rcol = sb("rcol", [P, 4])
        sq = sb("sq", [P, 2, T])
        psum = ctx.enter_context(nc.psum_tensor("psum", [P, 8, T], F32))
        cosb = sb("cosb", [P, T])
        sinb = sb("sinb", [P, T])

        evec = nc.dram_tensor("evec", (NH, NE), F32).ap()
        toep0 = nc.dram_tensor("toep0", (NH, P, 2 * P), F32).ap()
        toep1 = nc.dram_tensor("toep1", (2, NH, P, P), F32).ap()
        qkrow = nc.dram_tensor("qkrow", (2 * HG, T), F32).ap()
        frow = nc.dram_tensor("frow", (HG, G + 1, T), F32).ap()
        xsave = nc.dram_tensor("xsave", (P, KD * T), F32).ap()
        crow = nc.dram_tensor("crow", (2, CH, T), F32).ap()

        s_const = sem("s_const")
        s_xin = [sem(f"s_xin{c}") for c in range(4)]
        s_raw = [sem(f"s_raw{s}") for s in range(RAW)]
        s_out = sem("s_out")
        s_memset = sem("s_memset")
        s_go = sem("s_go")
        s_pe_go = sem("s_pe_go")
        hi_done = sem("hi_done")
        split_done = sem("split_done")
        blk_done = sem("blk_done")
        stat_mm = sem("stat_mm")
        v_half = sem("v_half")
        act_evac = sem("act_evac")
        x_sq = sem("x_sq")
        sq_acc = sem("sq_acc")
        out_mm = sem("out_mm")
        norm_sd = sem("norm_sd")
        norm_rcol = sem("norm_rcol")
        norm_mm = sem("norm_mm")
        h_full = sem("h_full")
        h_hi_done = sem("h_hi_done")
        h_lo_done = sem("h_lo_done")
        y_full = sem("y_full")
        y_hi_done = sem("y_hi_done")
        y_lo_done = sem("y_lo_done")
        x_upd = sem("x_upd")

        block = ctx.enter_context(nc.Block())
        OWN = {"pe": [blk_done, v_half, stat_mm, norm_mm, out_mm],
               "act": [act_evac, x_sq, norm_sd, h_hi_done, y_hi_done],
               "dve": [sq_acc, norm_rcol, h_full, h_lo_done, y_full, y_lo_done, x_upd], "pool": []}

        def own(engine, name):
            OWN[engine].append(sem(name))
            return OWN[engine][-1]

        with ExitStack() as stage:
            h_of = sb("h_of", [P, KD, T], F32, stage)

        with ExitStack() as stage:
            y_hi = sb("y_hi", [P, KE, T], F32R, stage)
            y_lo = sb("y_lo", [P, KE, T], F32R, stage)
            cv_c = sb("cv_c", [P, T], F32, stage)
            cv_u = sb("cv_u", [P, T], F32, stage)
            cv_z = sb("cv_z", [P, T], F32, stage)
            cv_b = sb("cv_b", [P, T], F32, stage)
            cv_v = sb("cv_v", [P, T + 2], F32, stage)
            cv_t = sb("cv_t", [P, T], F32, stage)
            adaw = sb("adaw", [P, 3 * D], F32, stage)
            adaacc = sb("adaacc", [P, 3 * D], F32, stage)
            oneh = sb("oneh", [33, NE], F32, stage)
            relt = sb("relt", [33, G * NH], F32, stage)
            esb = sb("esb", [NH, NE], F32, stage)
            cact = sb("cact", [P, KD], F32, stage)
        s_ada = sem("s_ada")
        s_evec = sem("s_evec")
        s_toep = sem("s_toep")
        cv_vd = own("dve", "cv_vd")
        cv_t0 = own("dve", "cv_t0")
        cv_t1 = own("dve", "cv_t1")
        cv_t2 = own("dve", "cv_t2")
        cv_t2b = own("dve", "cv_t2b")
        ada_raw = own("dve", "ada_raw")
        ada_mac = own("dve", "ada_mac")
        ada_out = own("dve", "ada_out")
        ada_sum = own("pe", "ada_sum")
        c_act = own("act", "c_act")
        e_mm = own("pe", "e_mm")
        e_sb = own("act", "e_sb")

        with ExitStack() as stage:
            ya_hi = sb("ya_hi", [P, KD, T], F32R, stage)
            ya_lo = sb("ya_lo", [P, KD, T], F32R, stage)
            biast = sb("biast", [P, HG, 2 * P], F32, stage)
            qkraw = sb("qkraw", [P, 4, T], F32, stage)
            qkn = sb("qkn", [P, 4, T], F32, stage)
            with ExitStack() as over:
                qksq_lo = sb("qksq_lo", [P, 4, T], F32R, over)
            nrmb = sb("nrmb", [P, 4, T], F32, stage)
            vt = sb("vt", [P, 4, HC], F32, stage)
            prob = sb("prob", [P, 7 * P], F32, stage)
            probT = sb("probT", [P, 7 * P], F32, stage)
            oacc = sb("oacc", [P, G, 2, T], F32, stage)
            fb = sb("fb", [P, (G + 1) * T], F32, stage)
            nmc = sb("nmc", [P, 4, HG], F32, stage)
            denc = sb("denc", [P, 4, HG], F32, stage)
            nrow = sb("nrow", [HG, G, T], F32, stage)
            drow = sb("drow", [HG, G, T], F32, stage)
            mrow = sb("mrow", [HG, T], F32, stage)
            srow = sb("srow", [2 * HG, T], F32, stage)
            zs = sb("zs", [P, 2, T], F32, stage)
            yt = sb("yt", [P, T], F32, stage)
            yu = sb("yu", [P, T], F32, stage)
            selt = sb("selt", [P, 4, 2 * HG], F32, stage)
            selr = sb("selr", [P, 4, 2 * HG], F32R, stage)
            gaint = sb("gaint", [P, 2 * G], F32, stage)
            fb1 = qkraw[:].rearrange("p a t -> p (a t)")
        s_sel = sem("s_sel")
        s_bias = sem("s_bias")
        s_qkw = sem("s_qkw")
        s_qkb = sem("s_qkb")
        s_fw = sem("s_fw")
        s_fs = sem("s_fs")
        s_fb = sem("s_fb")
        s_fb1 = sem("s_fb1")
        s_fsb = sem("s_fsb")
        s_fsb1 = sem("s_fsb1")
        gains = own("dve", "gains")
        qk_sq = own("act", "qk_sq")
        qksq_hi_done = own("dve", "qksq_hi_done")
        qksq_lo_done = own("dve", "qksq_lo_done")
        qk_stat = own("pe", "qk_stat")
        qk_sd = own("act", "qk_sd")
        qk_rstd = own("dve", "qk_rstd")
        qk_norm = own("dve", "qk_norm")
        sc_mm = own("pe", "sc_mm")
        sc_add = own("dve", "sc_add")
        sc_max = own("dve", "sc_max")
        sc_exp = own("act", "sc_exp")
        pt_mm = own("pe", "pt_mm")
        pt_cp = own("dve", "pt_cp")
        pv_mm = own("pe", "pv_mm")
        o_cp = own("dve", "o_cp")
        tr_mm = own("pe", "tr_mm")
        tr_cp = own("dve", "tr_cp")
        mg_max = own("dve", "mg_max")
        mg_exp = own("act", "mg_exp")
        mg_chain = own("dve", "mg_chain")
        mg_f = own("dve", "mg_f")
        ym_chain = own("dve", "ym_chain")
        ym_gate = own("dve", "ym_gate")

        with ExitStack() as stage:
            yl_hi = sb("yl_hi", [P, KE, T], F32R, stage)
            yl_lo = sb("yl_lo", [P, KE, T], F32R, stage)
            dect = sb("dect", [P, CH, T], F32, stage)
            trit = sb("trit", [P, P], F32, stage)
            pad = sb("pad", [P, 2, KC2 - 1 + T], F32, stage)
            tmp = sb("tmp", [P, 2, T], F32, stage)
            qk_hi = sb("qk_hi", [P, 4, T], F32R, stage)
            v_hi = sb("v_hi", [P, 4, HC], F32R, stage)
            ol = sb("ol", [P, 2, T], F32, stage)
            zl = sb("zl", [P, 2, T], F32, stage)
            with ExitStack() as over:
                wgt_lo = sb("wgt_lo", [P, 10 * P], F32R, over)
            wgt = sb("wgt", [P, 10 * P], F32, stage)
            nmb = sb("nmb", [P, T], F32, stage)
            emb = sb("emb", [P, T], F32, stage)
            argd = sb("argd", [P, 4, P], F32, stage)
            hc = sb("hc", [P, 2, T], F32, stage)
            lmod = sb("lmod", [P, 3 * KD], F32, stage)
            hcol = sb("hcol", [P, 4 * (KC2 + 1)], F32, stage)
            gcol = sb("gcol", [P, 2], F32, stage)
            gbc = sb("gbc", [64, 1], F32, stage)
            ccol = sb("ccol", [P, 4, CH], F32, stage)
            cch = sb("cch", [P, 4], F32, stage)
            g_i, g_f = wgt[0:CH, 0:T], wgt[0:CH, T:2 * T]
            g_b, g_m = argd[0:CH].rearrange("p a b -> p (a b)"), nmb[0:CH, :]
            g_c, g_max = hc[0:CH, 0, :], hc[0:CH, 1, :]
        s_rope = sem("s_rope")
        s_lc = sem("s_lc")
        s_hcol = sem("s_hcol")
        s_xsave = sem("s_xsave")
        s_xback = sem("s_xback")
        s_gcol = sem("s_gcol")
        s_crw = sem("s_crw")
        s_crb = sem("s_crb")
        s_gbc = sem("s_gbc")
        rope_v = own("dve", "rope_v")
        rope_a = own("act", "rope_a")
        l_mod = own("dve", "l_mod")
        g_act = own("act", "g_act")
        g_dve = own("dve", "g_dve")
        cc_mm = own("pe", "cc_mm")
        cc_cp = own("dve", "cc_cp")
        cvl = own("dve", "cvl")
        cvl_t = own("dve", "cvl_t")
        qk_silu = own("act", "qk_silu")
        qk_hi_done = own("act", "qk_hi_done")
        qk_lo_done = own("dve", "qk_lo_done")
        v_free = own("dve", "v_free")
        wgt_hi_done = own("act", "wgt_hi_done")
        wgt_lo_done = own("dve", "wgt_lo_done")
        rot_t = own("dve", "rot_t")
        rot_d = own("dve", "rot_d")
        w_arg = own("dve", "w_arg")
        w_exp = own("act", "w_exp")
        st_mm = own("pe", "st_mm")
        a_done = own("dve", "a_done")
        nv_mm = own("pe", "nv_mm")
        den_abs = own("act", "den_abs")
        den_max = own("dve", "den_max")
        den_rec = own("dve", "den_rec")
        hc_done = own("dve", "hc_done")
        mean_mm = own("pe", "mean_mm")
        w_sum = own("dve", "w_sum")
        w_sum_t = own("dve", "w_sum_t")
        h_sum = own("dve", "h_sum")
        sq_sum = own("dve", "sq_sum")
        cen = own("dve", "cen")
        c_sq = own("act", "c_sq")
        var_mm = own("pe", "var_mm")
        c_sd = own("act", "c_sd")
        c_rstd = own("dve", "c_rstd")
        n_gain = own("dve", "n_gain")
        n_o = own("dve", "n_o")

        V_ATT = CONV_B
        V_LAYER = V_ATT + ATT_B
        V_PER = CELL_B + GATE_B
        Y_ATT = KE
        Y_LAYER = Y_ATT + KD

        @block.sync
        def _(sp):
            def const(dst, src, s=s_const):
                sp.dma_start(dst, src).then_inc(s, 16)

            for c in range(4):
                sp.dma_start(xs[:, 2 * c:2 * c + 2, :],
                             x[2 * c:2 * c + 2].rearrange("c p t -> p c t")).then_inc(s_xin[c], 16)
            const(colt[:], cols)
            const(relt[0:NBUCKET, :], relb)
            const(oneh[:], onehot)
            const(idt[:], ident)

            def load(n, s):
                sp.dma_start(raw[:, s, :], wstream[ds(n, 1)].rearrange("a p n -> (a p) n"))\
                  .then_inc(s_raw[s], 16)

            for s in range(RAW):
                load(s, s)
            with sp.Fori(1, NB // RAW) as i:
                for s in range(RAW):
                    sp.wait_ge(split_done, RAW * i + s - RAW + 1)
                    load(RAW * i + s, s)
            for oc in range(KD):
                sp.wait_ge(h_full, after(4 * KD + oc))
                sp.dma_start(out[oc], xs[:, oc, :]).then_inc(s_out, 16)
            sp.wait_ge(s_out, 16 * KD)

        @block.gpsimd
        def _(pool):
            for i, (dst, value) in enumerate(((ones[:], 1.0), (zcol[:], 0.0), (onec[:], 1.0),
                                              (relt[NBUCKET:NBUCKET + 1, :], 1.0), (cv_v[:, 0:2], 0.0))):
                if i:
                    pool.wait_ge(s_memset, i)
                pool.memset(dst, value).then_inc(s_memset, 1)

            def split(n, s, free):
                t = s % SPL
                pool.wait_ge(s_raw[s], 16 * (n // RAW + 1) if isinstance(n, int) else free[1])
                if free[0] is not None:
                    pool.wait_ge(blk_done, free[0])
                pool.sem_inc(s_go, 1)
                pool.tensor_scalar(w_hi[:, t, :], raw[:, s, :], 1.0, 0.0, ALU.mult, ALU.add)\
                    .then_inc(hi_done, 1)
                pool.wait_ge(hi_done, n + 1)
                pool.tensor_tensor(w_lo[:, t, :], raw[:, s, :], w_hi[:, t, :].bitcast(F32), ALU.subtract)\
                    .then_inc(split_done, 1)

            for s in range(RAW):
                split(s, s, (after(s - SPL) if s >= SPL else None, None))
            with pool.Fori(1, NB // RAW) as i:
                for s in range(RAW):
                    split(RAW * i + s, s, (after(RAW * i + s - SPL), 16 * i + 16))

        @block.tensor
        def _(pe):
            for s in OWN["pe"]:
                pe.sem_inc(s, PRIME)

            def multiply(n, s, dst, k0=0, k1=KD):
                pe.wait_ge(split_done, n + 1)
                for k in range(k0, k1):
                    hi = w_hi[:, s, k * P:(k + 1) * P]
                    lo = w_lo[:, s, k * P:(k + 1) * P]
                    pe.matmul(dst, hi, h_hi[:, k, :], start=(k == 0), stop=False)
                    pe.matmul(dst, hi, h_lo[:, k, :], start=False, stop=False)
                    mm = pe.matmul(dst, lo, h_hi[:, k, :], start=False, stop=(k == KD - 1))
                if k1 == KD:
                    mm.then_inc(blk_done, 1)

            def values(n, half, evac, tokens):
                pe.wait_ge(split_done, n + 1)
                for j in range(4):
                    if half == 0 and j % 2 == 0:
                        pe.wait_ge(act_evac, after(evac + j // 2))
                    dst = psum[:, j // 2, (j % 2) * HC:(j % 2 + 1) * HC]
                    for k in range(4):
                        kk = 4 * half + k
                        first, last = kk == 0, kk == KD - 1
                        hi = w_hi[:, half, k * HC:(k + 1) * HC]
                        lo = w_lo[:, half, k * HC:(k + 1) * HC]
                        pe.matmul(dst, h_hi[:, kk, tokens(j)], hi, start=first and j % 2 == 0, stop=False,
                                  skip_group_check=True)
                        pe.matmul(dst, h_hi[:, kk, tokens(j)], lo, start=False, stop=False,
                                  skip_group_check=True)
                        mm = pe.matmul(dst, h_lo[:, kk, tokens(j)], hi, start=False,
                                       stop=last and j % 2 == 1, skip_group_check=True)
                    if half == 1 and j == 1:
                        mm.then_inc(v_half, 1)
                mm.then_inc(blk_done, 1)

            def stat(m):
                pe.wait_ge(sq_acc, after(SQ_ADD * m + SQ_ADD - 1))
                for b in range(4):
                    mm = pe.matmul(psum[:, STAT, b:b + 1], rstd[:, b * P:(b + 1) * P], ones[:, 0:1],
                                   start=True, stop=True)
                mm.then_inc(stat_mm, 1)
                pe.wait_ge(norm_rcol, after(m))
                for b in range(4):
                    mm = pe.matmul(psum[:, NORM, b * P:(b + 1) * P], rcol[:, b:b + 1].broadcast_to([P, P]),
                                   idt[:], start=True, stop=True)
                mm.then_inc(norm_mm, 1)

            def first_two(n, m):
                for b in range(2):
                    pe.wait_ge(split_done, n + b + 1)
                    for k in range(KD):
                        if b == 0:
                            pe.wait_ge(h_hi_done, after(KD * m + k))
                        w = slice(k * P, (k + 1) * P)
                        pe.matmul(psum[:, b, :], w_hi[:, b, w], h_hi[:, k, :], start=(k == 0), stop=False)
                        pe.matmul(psum[:, b, :], w_lo[:, b, w], h_hi[:, k, :], start=False, stop=False)
                for b in range(2):
                    for k in range(KD):
                        if b == 0:
                            pe.wait_ge(h_lo_done, after(KD * m + k))
                        mm = pe.matmul(psum[:, b, :], w_hi[:, b, k * P:(k + 1) * P], h_lo[:, k, :],
                                       start=False, stop=(k == KD - 1))
                    mm.then_inc(blk_done, 1)

            def out_block(n, s, pair, hi, lo, banks, free=None, last=False):
                pe.wait_ge(split_done, n + 1)
                for j in range(4):
                    if free is not None:
                        free(j)
                    dst = psum[:, banks[j], :]
                    for k in range(2):
                        w = slice((2 * j + k) * P, (2 * j + k + 1) * P)
                        y_h = hi[:, ds(2 * pair + k, 1), :].rearrange("p a t -> p (a t)")
                        y_l = lo[:, ds(2 * pair + k, 1), :].rearrange("p a t -> p (a t)")
                        pe.matmul(dst, w_hi[:, s, w], y_h, start=(free is not None and k == 0), stop=False)
                        pe.matmul(dst, w_hi[:, s, w], y_l, start=False, stop=False)
                        mm = pe.matmul(dst, w_lo[:, s, w], y_h, start=False, stop=(last and k == 1))
                    if last and j < 3:
                        mm.then_inc(out_mm, 1)
                mm.then_inc(blk_done, 1)

            def out_pairs(n, s, pair, count, hi, lo, banks):
                with pe.Fori(0, count) as i:
                    for j in range(2):
                        out_block(n + 2 * i + j, (s + j) % SPL, pair + 2 * i + j, hi, lo, banks)

            def out_last(n, pair, hi, lo, banks, y_last, m):
                pe.wait_ge(y_lo_done, after(y_last))
                out_block(n, 0, pair, hi, lo, banks[:4], last=True)
                out_block(n + 1, 1, pair, hi, lo, banks[4:], last=True)
                stat(m)

            pe.wait_ge(s_memset, 5)
            pe.wait_ge(s_const, 16 * 4)
            stat(0)

            at = 0
            for g in range(G):
                width = W0 if g == 0 else W1
                pe.matmul(psum[0:NH, 4 + g, 0:width], relt[:, g * NH:(g + 1) * NH], oneh[:, at:at + width],
                          start=True, stop=True).then_inc(e_mm, 1)
                at += width

            def conv_chunk(e, j0=0):
                for j in range(j0, 4):
                    pe.wait_ge(act_evac, after(4 * e + j - 4))
                    multiply(4 * e + j, j % SPL, psum[:, j, :])

            def modulation(half):
                pe.wait_ge(ada_mac, after(half * KD + KD - 1))
                pe.wait_ge(ada_out, after(half - 1))
                if half == 0:
                    pe.wait_ge(e_sb, after(G - 1))
                for c in range(3 * KD):
                    mm = pe.matmul(psum[:, MISC, c:c + 1], adaacc[:, c * P:(c + 1) * P], ones[:, 0:1],
                                   start=True, stop=True)
                mm.then_inc(ada_sum, 1)

            first_two(0, 0)
            conv_chunk(0, 2)
            with pe.Fori(1, KD) as e:
                conv_chunk(e)
            conv_chunk(KD)
            modulation(0)
            with pe.Fori(KD + 1, KE) as e:
                conv_chunk(e)

            def first_banks(j):
                pe.wait_ge(act_evac, after(CONV_B - 4 + j))

            def last_banks(j):
                if j == 3:
                    pe.wait_ge(ada_out, after(1))

            n = B_CONV_OUT
            pe.wait_ge(y_lo_done, after(KE - 3))
            out_block(n, 0, 0, y_hi, y_lo, CONV_OUT[:4], first_banks)
            out_pairs(n + 1, 1, 1, 3, y_hi, y_lo, CONV_OUT[:4])
            modulation(1)
            out_block(n + 7, 1, 0, y_hi, y_lo, CONV_OUT[4:], last_banks)
            out_pairs(n + 8, 0, 1, 3, y_hi, y_lo, CONV_OUT[4:])
            out_last(n + 14, 7, y_hi, y_lo, CONV_OUT, KE - 1, 1)


            def scores(u, g, h):
                c, base = h // 2, HD * (h % 2)
                q = qkn[base:base + HD, c, :]
                k = qkn[base:base + HD, 2 + c, :]
                pe.wait_ge(qk_norm, after(4 * u + 2 * c + 1))
                pe.wait_ge(sc_add, after(4 * u + h - 1))
                if g == 0:
                    pe.matmul(psum[:, 2, 0:P], q[:, 0:P], k[:, 0:P], start=True, stop=True)
                    pe.matmul(psum[:, 2, P:3 * P], q[:, P:2 * P], k[:, 0:2 * P], start=True, stop=True)
                    pe.matmul(psum[:, 3, 0:2 * P], q[:, 2 * P:3 * P], k[:, P:3 * P], start=True, stop=True)
                    mm = pe.matmul(psum[:, 3, 2 * P:4 * P], q[:, 3 * P:], k[:, 2 * P:], start=True, stop=True)
                else:
                    for r in range(4):
                        mm = pe.matmul(psum[:, 2, r * P:(r + 1) * P], q[:, r::4], k[:, r::4],
                                       start=True, stop=True)
                mm.then_inc(sc_mm, 1)

            def turn(u, g, h):
                pe.wait_ge(sc_exp, after(4 * u + h))
                pe.wait_ge(pt_cp, after(4 * u + h - 1))
                if h == 0:
                    pe.wait_ge(tr_cp, after(2 * u - 1))
                for t in range(7 if g == 0 else 4):
                    mm = pe.transpose(psum[:, 4 + t // 4, (t % 4) * P:(t % 4 + 1) * P],
                                      prob[:, t * P:(t + 1) * P], idt[:])
                mm.then_inc(pt_mm, 1)

            def weigh(u, g, h, v_evac):
                pe.wait_ge(pt_cp, after(4 * u + h))
                if h == 0:
                    pe.wait_ge(act_evac, after(v_evac))
                pe.wait_ge(o_cp, after(2 * u + h // 2 - 1))
                base = HD * (h % 2)
                for b in range(4):
                    dst = psum[base:base + HD, O, b * P:(b + 1) * P]
                    v = vt[:, b, h * HD:(h + 1) * HD]
                    if g == 0 and b > 0:
                        before = vt[:, b - 1, h * HD:(h + 1) * HD]
                        pe.matmul(dst, before, probT[:, (2 * b - 1) * P:2 * b * P], start=True, stop=False)
                        mm = pe.matmul(dst, v, probT[:, 2 * b * P:(2 * b + 1) * P], start=False, stop=True)
                    else:
                        mm = pe.matmul(dst, v, probT[:, b * P:(b + 1) * P], start=True, stop=True)
                mm.then_inc(pv_mm, 1)

            def turn_stats(u, sd_before):
                pe.wait_ge(qk_sd, after(sd_before))
                for b in range(4):
                    mm = pe.transpose(psum[0:HG, ROW, b * P:(b + 1) * P], nmc[:, b, :], idt[:])
                mm.then_inc(tr_mm, 1)
                for b in range(4):
                    mm = pe.transpose(psum[0:HG, 4, b * P:(b + 1) * P], denc[:, b, :], idt[:])
                mm.then_inc(tr_mm, 1)

            def qk_stats(u, tr_before):
                pe.wait_ge(tr_cp, after(tr_before))
                for c in range(4):
                    pe.wait_ge(qksq_lo_done, after(4 * u + c))
                    pe.matmul(psum[0:2 * HG, ROW, :], selr[:, c, :], qksq_hi[:, c, :],
                              start=(c == 0), stop=False)
                    mm = pe.matmul(psum[0:2 * HG, ROW, :], selr[:, c, :], qksq_lo[:, c, :],
                                   start=False, stop=(c == 3))
                mm.then_inc(qk_stat, 1)

            def att_chunk(i, s, k0=0, k1=KD):
                pe.wait_ge(act_evac, after(V_ATT + i - 2))
                multiply(B_ATT + i, s, psum[:, s, :], k0, k1)

            def att_values(i, half, g):
                tokens = (lambda j: slice(j * P, (j + 1) * P)) if g == 0 else (lambda j: slice(j, T, 4))
                values(B_ATT + i + half, half, V_ATT + i - 2, tokens)

            def att_unit(quad, g):
                p, pg, i = 3 * quad + g - 1, g - 1, 20 * quad + 6 * g
                pv = V_ATT + i - 1
                att_chunk(i, 0)
                att_chunk(i + 1, 1, 0, 4)
                scores(p, pg, 0)
                att_chunk(i + 1, 1, 4)
                scores(p, pg, 1)
                att_chunk(i + 2, 0, 0, 4)
                turn(p, pg, 0)
                att_chunk(i + 2, 0, 4)
                scores(p, pg, 2)
                turn(p, pg, 1)
                weigh(p, pg, 0, pv)
                att_chunk(i + 3, 1)
                scores(p, pg, 3)
                turn(p, pg, 2)
                weigh(p, pg, 1, pv)
                att_values(i + 4, 0, g)
                turn(p, pg, 3)
                weigh(p, pg, 2, pv)
                qk_stats(p + 1, 2 * p - 1)
                att_values(i + 4, 1, g)
                weigh(p, pg, 3, pv)
                turn_stats(p, p + 1)

            def att_last(quad, more):
                p, i = 3 * quad + 2, 20 * quad + 18
                pv = V_ATT + i - 1

                def out_part(pair):
                    def taken(j):
                        if j < 2:
                            pe.wait_ge(act_evac, after(V_ATT + ATT_B - 2 + j))
                    out_block(B_ATT_OUT + pair, pair % SPL, pair, ya_hi, ya_lo, ATT_OUT[:4],
                              taken if pair == 0 else None)

                att_chunk(i, 0)
                att_chunk(i + 1, 1, 0, 4)
                scores(p, 2, 0)
                att_chunk(i + 1, 1, 4)
                scores(p, 2, 1)
                if more:
                    att_chunk(i + 2, 0, 0, 4)
                turn(p, 2, 0)
                if more:
                    att_chunk(i + 2, 0, 4)
                else:
                    pe.wait_ge(y_lo_done, after(Y_ATT + KD - 3))
                    out_part(0)
                scores(p, 2, 2)
                turn(p, 2, 1)
                weigh(p, 2, 0, pv)
                if more:
                    att_chunk(i + 3, 1)
                else:
                    out_part(1)
                scores(p, 2, 3)
                turn(p, 2, 2)
                weigh(p, 2, 1, pv)
                if more:
                    att_chunk(i + 4, 0)
                turn(p, 2, 3)
                weigh(p, 2, 2, pv)
                if more:
                    att_chunk(i + 5, 1)
                weigh(p, 2, 3, pv)
                turn_stats(p, p)
                if more:
                    att_values(i + 6, 0, 0)
                    qk_stats(p + 1, 2 * p + 1)
                    att_values(i + 6, 1, 0)
                else:
                    out_part(2)

            first_two(B_ATT, 1)
            for j in (2, 3):
                att_chunk(j, j % 2)
            att_values(4, 0, 0)
            pe.wait_ge(gains, after(1))
            qk_stats(0, -1)
            att_values(4, 1, 0)
            att_unit(0, 1)
            with pe.Fori(0, NQUAD - 1) as quad:
                att_unit(quad, 2)
                att_last(quad, True)
                att_unit(quad + 1, 1)
            att_unit(NQUAD - 1, 2)
            att_last(NQUAD - 1, False)

            def taken(j):
                if j in (1, 3):
                    pe.wait_ge(tr_cp, after(6 * NQUAD - 1))
                elif j == 2:
                    pe.wait_ge(o_cp, after(6 * NQUAD - 1))

            out_block(B_ATT_OUT + 3, 1, 0, ya_hi, ya_lo, ATT_OUT[4:], taken)
            for pair in (1, 2):
                out_block(B_ATT_OUT + 3 + pair, (3 + pair) % SPL, pair, ya_hi, ya_lo, ATT_OUT[4:])
            out_last(B_ATT_OUT + 6, 3, ya_hi, ya_lo, ATT_OUT, Y_ATT + KD - 1, 2)

            def similar(U):
                pe.wait_ge(qk_lo_done, after(4 * U + 3))
                pe.wait_ge(a_done, after(NP * (U - 1) + NP - 1))
                for st in range(4):
                    bank, col, _ = S_AT[st]
                    width = T - st * P
                    dst, s_tile = psum[:, bank, col:col + width], slice(st * P, (st + 1) * P)
                    for c in range(2):
                        k_h, k_l = qk_hi[:, 2 + c, s_tile], qk_lo[:, 2 + c, s_tile]
                        q_h, q_l = qk_hi[:, c, st * P:], qk_lo[:, c, st * P:]
                        pe.matmul(dst, k_h, q_h, start=(c == 0), stop=False)
                        pe.matmul(dst, k_h, q_l, start=False, stop=False)
                        mm = pe.matmul(dst, k_l, q_h, start=False, stop=(c == 1))
                mm.then_inc(st_mm, 1)

            def numerator(U, mlstm, H):
                pe.wait_ge(hc_done, after(U - 1))
                pe.wait_ge(cen, after(2 * U - 1))
                for c in range(2):
                    for st in range(4):
                        if c == 0 and st < NP:
                            pe.wait_ge(wgt_lo_done, after(NP * U + st))
                        dst, w = psum[:, NUM + c, st * P:], slice(S_AT[st][2], S_AT[st][2] + T - st * P)
                        v_h, v_l = v_hi[:, st, c * P:(c + 1) * P], v_lo[:, st, c * P:(c + 1) * P]
                        pe.matmul(dst, v_h, wgt_hi[:, w], start=(st == 0), stop=False, skip_group_check=True)
                        pe.matmul(dst, v_h, wgt_lo[:, w], start=False, stop=False, skip_group_check=True)
                        mm = pe.matmul(dst, v_l, wgt_hi[:, w], start=False, stop=(st == 3),
                                       skip_group_check=True)
                if mlstm:
                    pe.wait_ge(w_sum, after(H))
                    mm = pe.matmul(psum[:, NUM + 2, :], ones[:], nmb[:], start=True, stop=True)
                mm.then_inc(nv_mm, 1)

            def mean(U):
                pe.wait_ge(h_sum, after(U))
                pe.matmul(psum[:, AUX, :], ones[:], sq[:, 0, :], start=True, stop=True).then_inc(mean_mm, 1)

            def variance(U):
                pe.wait_ge(sq_sum, after(U))
                pe.matmul(psum[:, 2, :], ones[:], sq[:, 0, :], start=True, stop=True).then_inc(var_mm, 1)

            def layer(l):
                n0, v0, u0 = B_LAYER + LAYER_B * l, V_LAYER + V_PER * l, NCELL * l

                def chunk(i, s, k0=0, k1=KD):
                    pe.wait_ge(act_evac, after(v0 + i - 2))
                    multiply(n0 + i, s, psum[:, s, :], k0, k1)

                def cell_values(i, half):
                    values(n0 + i + half, half, v0 + i - 2, lambda j: slice(j * P, (j + 1) * P))

                def unit(j, i, mlstm, before):
                    U = u0 + j - 1
                    if before:
                        similar(U)
                        chunk(i, 0)
                        numerator(U, not mlstm, CH * l + before[0])
                        chunk(i + 1, 1)
                        if mlstm:
                            mean(U)
                    chunk(i + 2, 0, 0, 4)
                    if before and not mlstm:
                        mean(U)
                    chunk(i + 2, 0, 4)
                    chunk(i + 3, 1)
                    if before:
                        variance(U)
                    cell_values(i + 4, 0)
                    cell_values(i + 4, 1)
                    for m in range(4 if mlstm else 2):
                        if m < 2:
                            pe.wait_ge(v_free, after(2 * (U + 1) + m))
                        chunk(i + 6 + m, m % 2)
                        if m == 0 and not before:
                            pe.wait_ge(g_dve, after(G_DVE * l + 3))
                            pe.sem_inc(s_pe_go, 1)
                            for b in range(4):
                                mm = pe.transpose(psum[:, AUX, b * CH:(b + 1) * CH],
                                                  g_c[:, b * P:(b + 1) * P], idt[0:CH, 0:CH])
                            mm.then_inc(cc_mm, 1)

                first_two(n0, 2 + l)
                for b in range(GATE_B):
                    pe.wait_ge(split_done, n0 + 2 + b + 1)
                    for k in range(4):
                        kk = 4 * b + k
                        hi = w_hi[:, b, k * P:(k + 1) * P]
                        lo = w_lo[:, b, k * P:(k + 1) * P]
                        pe.matmul(psum[:, GATE, :], hi, h_hi[:, kk, :], start=(kk == 0), stop=False)
                        pe.matmul(psum[:, GATE, :], hi, h_lo[:, kk, :], start=False, stop=False)
                        mm = pe.matmul(psum[:, GATE, :], lo, h_hi[:, kk, :], start=False, stop=(kk == KD - 1))
                    mm.then_inc(blk_done, 1)
                unit(0, GATE_B, True, None)
                unit(1, GATE_B + 10, False, (0,))
                with pe.Fori(1, CH) as h:
                    unit(2 * h, GATE_B + 18 * h, True, (h - 1,))
                    unit(2 * h + 1, GATE_B + 18 * h + 10, False, (h,))
                U, n = u0 + NCELL - 1, n0 + GATE_B + CELL_B

                def first_banks(j):
                    if j < 2:
                        pe.wait_ge(act_evac, after(v0 + V_PER - 2 + j))
                    else:
                        pe.wait_ge(a_done, after(NP * U + NP - 1))

                def last_banks(j):
                    if j == 0:
                        pe.wait_ge(c_sd, after(U))
                    elif j < 3:
                        pe.wait_ge(hc_done, after(U))
                    else:
                        pe.wait_ge(cen, after(2 * U + 1))

                similar(U)
                pe.wait_ge(y_lo_done, after(Y_LAYER + KE * l + KE - 3))
                out_block(n, 0, 0, yl_hi, yl_lo, LAYER_OUT[:4], first_banks)
                numerator(U, False, None)
                out_block(n + 1, 1, 1, yl_hi, yl_lo, LAYER_OUT[:4])
                mean(U)
                out_block(n + 2, 0, 2, yl_hi, yl_lo, LAYER_OUT[:4])
                variance(U)
                out_pairs(n + 3, 1, 3, 2, yl_hi, yl_lo, LAYER_OUT[:4])
                out_block(n + 7, 1, 0, yl_hi, yl_lo, LAYER_OUT[4:], last_banks)
                out_pairs(n + 8, 0, 1, 3, yl_hi, yl_lo, LAYER_OUT[4:])
                out_last(n + 14, 7, yl_hi, yl_lo, LAYER_OUT, Y_LAYER + KE * l + KE - 1, 3 + l)

            with pe.Fori(0, NL) as l:
                layer(l)

        @block.scalar
        def _(act):
            for s in OWN["act"]:
                act.sem_inc(s, PRIME)

            def root(m):
                act.wait_ge(stat_mm, after(m))
                act.activation(rcol[:], psum[:, STAT, 0:4], ACT.Sqrt, scale=1.0 / D, bias=EPS)\
                   .then_inc(norm_sd, 1)

            def norm_split(m, shift):
                for k in range(KD):
                    act.wait_ge(h_full, after(KD * m + k))
                    act.activation(h_hi[:, k, :], h_of[:, k, :], ACT.Identity, bias=shift[:, k:k + 1])\
                       .then_inc(h_hi_done, 1)

            def square(m, oc):
                if oc >= 3:
                    act.wait_ge(sq_acc, after(SQ_ADD * m + oc - 3))
                act.activation(rstd[:] if oc == 0 else sq[:, oc % 2, :], xs[:, oc, :], ACT.Square)\
                   .then_inc(x_sq, 1)

            def squares(m):
                for oc in range(KD):
                    act.wait_ge(x_upd, after(KD * (m - 1) + oc))
                    square(m, oc)
                root(m)

            def evac(n, dst, src, func=ACT.Copy):
                act.wait_ge(blk_done, after(n))
                act.activation(dst, src, func).then_inc(act_evac, 1)

            for c in range(KD):
                act.wait_ge(s_xin[c // 2], 16)
                square(0, c)
            root(0)
            act.wait_ge(s_memset, 5)
            norm_split(0, zcol)
            act.dma_start(sinb[:].bitcast(I32), bass.AP(pos.tensor, 0, [[0, P], [1, T]])).then_inc(s_rope, 16)
            act.wait_ge(s_const, 16 * 4)
            act.activation(cact[:], colt[:, C_C:C_C + KD], ACT.Silu).then_inc(c_act, 1)
            at = 0
            for g in range(G):
                width = W0 if g == 0 else W1
                act.wait_ge(e_mm, after(g))
                act.activation(esb[:, at:at + width], psum[0:NH, 4 + g, 0:width], ACT.Copy).then_inc(e_sb, 1)
                at += width
            act.wait_ge(e_sb, after(G - 1))
            act.dma_start(evec, esb[:]).then_inc(s_evec, 16)
            act.wait_ge(s_evec, 16)
            act.dma_start(toep0, bass.AP(evec.tensor, P - 1, [[NE, NH], [-1, P], [1, 2 * P]]))\
               .then_inc(s_toep, 16)
            for g in range(2):
                act.dma_start(toep1[g], bass.AP(evec.tensor, W0 + g * W1 + P - 1, [[NE, NH], [-1, P], [1, P]]))\
                   .then_inc(s_toep, 16)

            act.wait_ge(rope_v, after(ROPE_R))
            act.activation(sinb[:], cosb[:], ACT.Sin).then_inc(rope_a, 1)
            act.wait_ge(rope_a, after(0))
            act.activation(cosb[:], cosb[:], ACT.Sin, scale=0.5).then_inc(rope_a, 1)

            with act.Fori(0, KE) as e:
                act.wait_ge(ada_mac, after(e - 1))
                act.dma_start(adaw[:], wada[ds(e, 1)].rearrange("a p n -> (a p) n")).then_inc(s_ada, 16)
                act.wait_ge(cv_vd, after(e - 1))
                evac(4 * e, cv_c[:], psum[:, 0, :])
                evac(4 * e + 1, cv_u[:], psum[:, 1, :])
                act.wait_ge(y_full, after(e - 1))
                evac(4 * e + 2, cv_z[:], psum[:, 2, :], ACT.Silu)
                evac(4 * e + 3, cv_b[:], psum[:, 3, :])
                act.wait_ge(y_full, after(e))
                act.activation(y_hi[:, ds(e, 1), :].rearrange("p a t -> p (a t)"), cv_t[:], ACT.Copy)\
                   .then_inc(y_hi_done, 1)
            squares(1)

            norm_split(1, zcol)
            act.dma_start(xsave, xs[:].rearrange("p k t -> p (k t)")).then_inc(s_xsave, 16)
            act.wait_ge(h_lo_done, after(2 * KD - 1))
            act.dma_start(selt[:], sel).then_inc(s_sel, 16)

            def bias_tiles(u, quad, g):
                act.wait_ge(sc_add, after(4 * u - 1))
                src = (toep0 if g == 0 else toep1[g - 1])[ds(HG * quad, HG)]
                act.dma_start(biast[:, :, 0:2 * P if g == 0 else P], src.rearrange("h p n -> p h n"))\
                   .then_inc(s_bias, 16)

            def norm_rows_out(u):
                act.wait_ge(qk_rstd, after(u))
                act.dma_start(qkrow, srow[:]).then_inc(s_qkw, 16)

            def norm_rows_in(u):
                act.wait_ge(s_qkw, 16 * u + 16)
                for half in range(2):
                    act.dma_start(nrmb[HD * half:HD * (half + 1), :, :],
                                  bass.AP(qkrow.tensor, half * T, [[0, HD], [2 * T, 4], [1, T]]))\
                       .then_inc(s_qkb, 16)

            def qk_out(u, i, c):
                act.wait_ge(qk_norm, after(4 * (u - 1) + 3))
                evac(B_ATT + i, qkraw[:, c, :], psum[:, c % 2, :])
                act.wait_ge(act_evac, after(V_ATT + i))
                act.activation(nrmb[:, c, :], qkraw[:, c, :], ACT.Square).then_inc(qk_sq, 1)

            def qk_root(u):
                act.wait_ge(qk_stat, after(u))
                act.activation(srow[:], psum[0:2 * HG, ROW, :], ACT.Sqrt, scale=1.0 / HD, bias=EPS)\
                   .then_inc(qk_sd, 1)

            def v_out(u, i):
                act.wait_ge(pv_mm, after(4 * (u - 1) + 3))
                for b in range(2):
                    if b == 0:
                        act.wait_ge(v_half, after(u))
                    else:
                        act.wait_ge(blk_done, after(B_ATT + i + 1))
                    act.activation(vt[:, 2 * b:2 * b + 2, :].rearrange("p a n -> p (a n)"), psum[:, b, :],
                                   ACT.Copy).then_inc(act_evac, 1)

            def exps(u, g, h):
                act.wait_ge(sc_max, after(4 * u + h))
                if h == 0:
                    act.wait_ge(tr_mm, after(2 * u - 1))
                at = 0
                for b in range(4):
                    width = 2 * P if g == 0 and b > 0 else P
                    e = act.activation(prob[:, at:at + width], prob[:, at:at + width], ACT.Exp,
                                       bias=nmc[:, b, h:h + 1], accum_out=denc[:, b, h:h + 1])
                    at += width
                e.then_inc(sc_exp, 1)

            def weights_out(quad):
                act.wait_ge(mg_exp, after(quad))
                act.dma_start(frow[:, 0:G], nrow[:]).then_inc(s_fw, 16)

            def sums_out(quad):
                act.wait_ge(mg_f, after(quad))
                act.dma_start(frow[:, G], mrow[:]).then_inc(s_fs, 16)

            def head_rows(quad, c, row, rows, dst, done):
                for half in range(2):
                    act.dma_start(dst[HD * half:HD * (half + 1), row * T:(row + rows) * T],
                                  bass.AP(frow.tensor, ((2 * c + half) * (G + 1) + row) * T,
                                          [[0, HD], [1, rows * T]])).then_inc(done, 16)

            def weights_in(quad, c, dst=fb[:], done=s_fb):
                act.wait_ge(s_fw, 16 * quad + 16)
                if done is s_fb:
                    act.wait_ge(y_full, after(Y_ATT + 2 * quad + c - 1))
                else:
                    act.wait_ge(qk_norm, after(12 * NQUAD - 1))
                head_rows(quad, c, 0, G, dst, done)

            def sums_in(quad, c, dst=fb[:], done=s_fsb):
                act.wait_ge(s_fs, 16 * quad + 16)
                head_rows(quad, c, G, 1, dst, done)

            def att_unit(quad, g, merge):
                p, pg, u, i = 3 * quad + g - 1, g - 1, 3 * quad + g, 20 * quad + 6 * g
                norm_rows_in(p)
                bias_tiles(p, quad, pg)
                if merge:
                    sums_out(quad - 1)
                qk_out(u, i, 0)
                exps(p, pg, 0)
                if merge:
                    weights_in(quad - 1, 0)
                    sums_in(quad - 1, 0)
                qk_out(u, i + 1, 1)
                exps(p, pg, 1)
                qk_out(u, i + 2, 2)
                exps(p, pg, 2)
                qk_out(u, i + 3, 3)
                if merge:
                    weights_in(quad - 1, 1)
                    sums_in(quad - 1, 1)
                exps(p, pg, 3)
                qk_root(u)
                norm_rows_out(u)
                v_out(u, i + 4)

            def att_last(quad, more):
                p, i = 3 * quad + 2, 20 * quad + 18
                norm_rows_in(p)
                bias_tiles(p, quad, 2)
                act.wait_ge(y_full, after(Y_ATT + 2 * quad - 1))
                evac(B_ATT + i, zs[:, 0, :], psum[:, 0, :], ACT.Silu)
                exps(p, 2, 0)
                evac(B_ATT + i + 1, zs[:, 1, :], psum[:, 1, :], ACT.Silu)
                exps(p, 2, 1)
                if more:
                    qk_out(p + 1, i + 2, 0)
                exps(p, 2, 2)
                if more:
                    qk_out(p + 1, i + 3, 1)
                exps(p, 2, 3)
                if more:
                    qk_out(p + 1, i + 4, 2)
                    qk_out(p + 1, i + 5, 3)
                act.wait_ge(mg_max, after(quad))
                act.activation(nrow[:], nrow[:], ACT.Exp).then_inc(mg_exp, 1)
                weights_out(quad)
                if more:
                    qk_root(p + 1)
                    v_out(p + 1, i + 6)
                    norm_rows_out(p + 1)

            for j in range(4):
                qk_out(0, j, j)
            qk_root(0)
            norm_rows_out(0)
            v_out(0, 4)
            act.wait_ge(s_toep, 48)
            att_unit(0, 1, False)
            with act.Fori(0, NQUAD - 1) as quad:
                att_unit(quad, 2, False)
                att_last(quad, True)
                att_unit(quad + 1, 1, True)
            att_unit(NQUAD - 1, 2, False)
            att_last(NQUAD - 1, False)
            weights_in(NQUAD - 1, 0)
            weights_in(NQUAD - 1, 1, fb1, s_fb1)
            sums_out(NQUAD - 1)
            sums_in(NQUAD - 1, 0)
            sums_in(NQUAD - 1, 1, fb1, s_fsb1)
            act.dma_start(xs[:].rearrange("p k t -> p (k t)"), xsave).then_inc(s_xback, 16)

            act.wait_ge(y_lo_done, after(Y_LAYER - 1))
            act.dma_start(dect[:], decay).then_inc(s_lc, 16)
            act.dma_start(trit[:], tri).then_inc(s_lc, 16)
            squares(2)

            def layer(l):
                n0, v0, u0 = B_LAYER + LAYER_B * l, V_LAYER + V_PER * l, NCELL * l
                act.wait_ge(g_dve, after(G_DVE * l - 1))
                act.dma_start(gbc[:], gatecols[ds(l, 1)].rearrange("a p n -> (a p) n")).then_inc(s_gbc, 16)
                norm_split(2 + l, lmod)
                act.dma_start(xsave, xs[:].rearrange("p k t -> p (k t)")).then_inc(s_xsave, 16)

                a0 = G_ACT * l

                def gates_out():
                    act.wait_ge(s_gbc, 16 * l + 16)
                    act.wait_ge(blk_done, after(n0 + 3))
                    act.activation(g_i, psum[0:CH, GATE, :], ACT.Identity, bias=gbc[0:CH, :]).then_inc(act_evac, 1)
                    act.activation(g_f, psum[32:32 + CH, GATE, :], ACT.Identity, bias=gbc[32:32 + CH, :])\
                       .then_inc(act_evac, 1)

                def gate_rows():
                    act.wait_ge(act_evac, after(v0 + 3))
                    act.activation(g_b, g_f, ACT.Abs).then_inc(g_act, 1)
                    act.wait_ge(g_act, after(a0))
                    act.activation(g_b, g_b, ACT.Exp, scale=-1.0).then_inc(g_act, 1)
                    act.wait_ge(g_act, after(a0 + 1))
                    act.activation(g_b, g_b, ACT.Ln, bias=1.0).then_inc(g_act, 1)

                def cell_squares(U):
                    for c in range(2):
                        act.wait_ge(cen, after(2 * U + c))
                        act.activation(sq[:, c, :], hc[:, c, :], ACT.Square).then_inc(c_sq, 1)

                def cell_root(U):
                    act.wait_ge(var_mm, after(U))
                    act.activation(rstd[:], psum[:, 2, :], ACT.Sqrt, scale=1.0 / HC, bias=EPS).then_inc(c_sd, 1)

                def cell_high(U, y0, at):
                    for c in range(2):
                        act.wait_ge(y_full, after(y0 + c))
                        act.activation(yl_hi[:, ds(at + c, 1), :].rearrange("p a t -> p (a t)"), hc[:, c, :],
                                       ACT.Copy).then_inc(y_hi_done, 1)

                def gains_in(U):
                    act.wait_ge(n_gain, after(2 * U - 1))
                    act.dma_start(gcol[:], gncols[ds(U, 1)].rearrange("a p n -> (a p) n")).then_inc(s_gcol, 16)

                def v_out(i, U):
                    act.wait_ge(nv_mm, after(U - 1))
                    for b in range(2):
                        if b == 0:
                            act.wait_ge(v_half, after(G * NQUAD + U))
                        else:
                            act.wait_ge(blk_done, after(n0 + i + 1))
                        act.activation(v_hi[:, 2 * b:2 * b + 2, :].rearrange("p a n -> p (a n)"),
                                       psum[:, b, :], ACT.Copy).then_inc(act_evac, 1)

                def silu(H, c):
                    act.wait_ge(cvl, after(4 * H + c))
                    act.activation(tmp[:, c % 2, :], tmp[:, c % 2, :], ACT.Silu).then_inc(qk_silu, 1)

                def qk_high(U, c, ready, value):
                    act.wait_ge(ready, value)
                    act.wait_ge(st_mm, after(U - 1))
                    act.activation(qk_hi[:, c, :], tmp[:, c % 2, :], ACT.Copy).then_inc(qk_hi_done, 1)

                def weights_high(U):
                    act.wait_ge(st_mm, after(U))
                    for i, (_, w0, w1) in enumerate(S_PIECES):
                        act.wait_ge(a_done, after(NP * U + i))
                        act.activation(wgt_hi[:, w0:w1], wgt[:, w0:w1], ACT.Copy).then_inc(wgt_hi_done, 1)

                def mlstm(h, i, before):
                    H, U, yb = CH * l + h, u0 + 2 * h, Y_LAYER + KE * l + 4 * h
                    act.wait_ge(cvl, after(4 * H - 1))
                    act.dma_start(hcol[:], headcols[ds(H, 1)].rearrange("a p n -> (a p) n")).then_inc(s_hcol, 16)
                    if before:
                        gains_in(U - 1)
                        weights_high(U - 1)
                    act.wait_ge(rot_d, after(2 * H - 1))
                    first = i if before else 0
                    evac(n0 + first, pad[:, 0, KC2 - 1:], psum[:, 0, :])
                    evac(n0 + first + 1, pad[:, 1, KC2 - 1:], psum[:, 1, :])
                    if not before:
                        gates_out()

                    def q_or_k(c):
                        silu(H, c)
                        qk_high(U, c, qk_silu, after(4 * H + c))

                    q_or_k(0)
                    q_or_k(1)
                    if before:
                        cell_squares(U - 1)
                    else:
                        gate_rows()
                    evac(n0 + i + 2, pad[:, 0, KC2 - 1:], psum[:, 0, :])
                    q_or_k(2)
                    evac(n0 + i + 3, pad[:, 1, KC2 - 1:], psum[:, 1, :])
                    if before:
                        cell_root(U - 1)
                    q_or_k(3)
                    v_out(i + 4, U)
                    if before is False:
                        act.wait_ge(g_dve, after(G_DVE * l + G_DVE - 1))
                        act.activation(g_m, g_m, ACT.Exp, scale=-1.0).then_inc(g_act, 1)
                        act.wait_ge(g_act, after(a0 + 3))
                        act.dma_start(crow[0], g_f).then_inc(s_crw, 16)
                        act.dma_start(crow[1], g_m).then_inc(s_crw, 16)
                    evac(n0 + i + 6, ol[:, 0, :], psum[:, 0, :], ACT.Sigmoid)
                    evac(n0 + i + 7, ol[:, 1, :], psum[:, 1, :], ACT.Sigmoid)
                    act.wait_ge(s_crw, 32 * l + 32)
                    act.wait_ge(den_max, after(H - 1))
                    act.wait_ge(w_arg, after(H - 1))
                    for r, dst in ((0, nmb), (1, emb)):
                        act.dma_start(dst[:], crow[r][ds(h, 1), :].rearrange("a t -> (a t)").partition_broadcast(P))\
                           .then_inc(s_crb, 16)
                    if before:
                        cell_high(U - 1, yb - 2, KD + 2 * (h - 1))
                    evac(n0 + i + 8, zl[:, 0, :], psum[:, 0, :], ACT.Silu)
                    evac(n0 + i + 9, zl[:, 1, :], psum[:, 1, :], ACT.Silu)
                    act.wait_ge(w_arg, after(H))
                    act.wait_ge(nv_mm, after(U - 1))
                    for st in range(4):
                        w0 = S_AT[st][2]
                        e = act.activation(wgt[:, w0:w0 + P], argd[:, st, :], ACT.Exp, bias=cch[:, st:st + 1])
                        if st < 3:
                            act.activation(wgt[:, w0 + P:w0 + T - st * P], nmb[:, (st + 1) * P:], ACT.Exp,
                                           bias=cch[:, st:st + 1])
                    e.then_inc(w_exp, 1)

                def retention(h, i):
                    H, U, yb = CH * l + h, u0 + 2 * h + 1, Y_LAYER + KE * l + 4 * h + 2
                    gains_in(U - 1)
                    weights_high(U - 1)
                    act.wait_ge(cvl, after(4 * H + 3))
                    evac(n0 + i, pad[:, 0, KC2 - 1:], psum[:, 0, :])
                    act.wait_ge(nv_mm, after(U - 1))
                    act.activation(rstd[:], psum[:, NUM + 2, :], ACT.Abs).then_inc(den_abs, 1)
                    evac(n0 + i + 1, pad[:, 1, KC2 - 1:], psum[:, 1, :])
                    for c in range(2):
                        qk_high(U, c, rot_t, after(7 * 2 * H + 3 * c + 2))
                    cell_squares(U - 1)
                    act.wait_ge(rot_d, after(2 * H))
                    evac(n0 + i + 2, pad[:, 0, KC2 - 1:], psum[:, 0, :])
                    evac(n0 + i + 3, pad[:, 1, KC2 - 1:], psum[:, 1, :])
                    cell_root(U - 1)
                    for c in range(2):
                        qk_high(U, 2 + c, rot_t, after(7 * (2 * H + 1) + 3 * c + 2))
                    v_out(i + 4, U)
                    act.wait_ge(y_full, after(yb - 1))
                    evac(n0 + i + 6, zl[:, 0, :], psum[:, 0, :], ACT.Silu)
                    cell_high(U - 1, yb - 2, 2 * h)
                    evac(n0 + i + 7, zl[:, 1, :], psum[:, 1, :], ACT.Silu)

                mlstm(0, GATE_B, False)
                retention(0, GATE_B + 10)
                with act.Fori(1, CH) as h:
                    mlstm(h, GATE_B + 18 * h, True)
                    retention(h, GATE_B + 18 * h + 10)
                U = u0 + NCELL - 1
                gains_in(U)
                weights_high(U)
                act.wait_ge(nv_mm, after(U))
                act.dma_start(xs[:].rearrange("p k t -> p (k t)"), xsave).then_inc(s_xback, 16)
                cell_squares(U)
                cell_root(U)
                cell_high(U, Y_LAYER + KE * l + KE - 2, KE - 2)
                squares(3 + l)

            with act.Fori(0, NL) as l:
                layer(l)

        @block.vector
        def _(dve):
            for s in OWN["dve"]:
                dve.sem_inc(s, PRIME)

            def norm_root(m):
                dve.wait_ge(norm_sd, after(m))
                dve.reciprocal(rcol[:], rcol[:]).then_inc(norm_rcol, 1)
                dve.wait_ge(norm_mm, after(m))

            def norm(m, gain, shift):
                norm_root(m)
                for k in range(KD):
                    dve.scalar_tensor_tensor(h_of[:, k, :], xs[:, k, :], gain[:, k:k + 1],
                                             psum[:, NORM, :], ALU.mult, ALU.mult).then_inc(h_full, 1)
                for k in range(KD):
                    dve.wait_ge(h_hi_done, after(KD * m + k))
                    dve.scalar_tensor_tensor(h_lo[:, k, :], h_of[:, k, :], shift[:, k:k + 1],
                                             h_hi[:, k, :].bitcast(F32), ALU.add, ALU.subtract)\
                       .then_inc(h_lo_done, 1)

            def update(st, oc, gate, n_last, banks):
                if oc % 4 < 3:
                    dve.wait_ge(out_mm, after(OUT_MM * st + 3 * (oc // 4) + oc % 4))
                else:
                    dve.wait_ge(blk_done, after(n_last + oc // 4))
                dve.scalar_tensor_tensor(xs[:, oc, :], psum[:, banks[oc], :], gate[:, oc:oc + 1], xs[:, oc, :],
                                         ALU.mult, ALU.add).then_inc(x_upd, 1)

            def add_square(m, oc):
                dve.wait_ge(x_sq, after(KD * m + oc))
                dve.tensor_tensor(rstd[:], rstd[:], sq[:, oc % 2, :], ALU.add).then_inc(sq_acc, 1)
                dve.wait_ge(sq_acc, after(SQ_ADD * m + oc - 1))

            def updates(st, gate, n_last, banks):
                for oc in range(KD):
                    update(st, oc, gate, n_last, banks)
                    if oc >= 2:
                        add_square(st + 1, oc - 1)
                add_square(st + 1, KD - 1)

            def rope(i, instruction):
                instruction.then_inc(rope_v, 1)
                dve.wait_ge(rope_v, after(i))

            dve.wait_ge(s_const, 16 * 4)
            dve.wait_ge(s_memset, 5)
            for oc in range(1, SQ_ADD + 1):
                add_square(0, oc)
            for c in range(4):
                dve.wait_ge(s_xin[c], 16)
            norm(0, colt[:, C_NORM:C_NORM + KD], zcol)
            dve.wait_ge(s_rope, 16)
            rope(0, dve.tensor_copy(cosb[:], sinb[:].bitcast(I32)))
            rope(1, dve.tensor_scalar(cosb[:], cosb[:], colt[:, C_FREQ:C_FREQ + 1], None, ALU.mult))
            rope(2, dve.tensor_scalar(sinb[:], cosb[:], 1.0 / (2 * math.pi), ROUND, ALU.mult, ALU.add))
            rope(3, dve.tensor_scalar(sinb[:], sinb[:], ROUND, None, ALU.subtract))
            rope(4, dve.scalar_tensor_tensor(cosb[:], sinb[:], -TWO_PI[0], cosb[:], ALU.mult, ALU.add))
            rope(5, dve.scalar_tensor_tensor(cosb[:], sinb[:], -TWO_PI[1], cosb[:], ALU.mult, ALU.add))
            rope(6, dve.scalar_tensor_tensor(cosb[:], sinb[:], -TWO_PI[2], cosb[:], ALU.mult, ALU.add))
            rope(7, dve.tensor_scalar(cosb[:], cosb[:], PI_BELOW, -PI_BELOW, ALU.min, ALU.max))
            dve.wait_ge(rope_a, after(1))
            rope(8, dve.scalar_tensor_tensor(cosb[:], cosb[:], -2.0, cosb[:], ALU.mult, ALU.mult))
            rope(9, dve.tensor_scalar(cosb[:], cosb[:], 1.0, None, ALU.add))
            dve.wait_ge(c_act, after(0))

            def modulation(half):
                dve.wait_ge(ada_sum, after(half))
                m = mods[:, half, :]
                b0 = C_ADAB + half * 3 * KD
                dve.tensor_tensor(m, psum[:, MISC, 0:3 * KD], colt[:, b0:b0 + 3 * KD], ALU.add)\
                   .then_inc(ada_raw, 1)
                dve.wait_ge(ada_raw, after(half))
                g0 = C_NORM + (2 + half) * KD
                dve.scalar_tensor_tensor(m[:, KD:2 * KD], m[:, KD:2 * KD], 1.0, colt[:, g0:g0 + KD],
                                         ALU.add, ALU.mult).then_inc(ada_out, 1)

            def conv_chunk(e, half, first):
                dve.wait_ge(act_evac, after(4 * e + 1))
                dve.tensor_tensor(cv_v[:, 2:], cv_c[:], cv_u[:], ALU.mult).then_inc(cv_vd, 1)
                dve.wait_ge(cv_vd, after(e))
                dve.wait_ge(y_hi_done, after(e - 1))
                dve.wait_ge(y_lo_done, after(e - 1))

                def tap(k):
                    return colt[:, ds(C_CONVW + k * KE + e, 1)]

                dve.tensor_scalar(cv_t[:], cv_v[:, 2:], tap(2), None, ALU.mult).then_inc(cv_t0, 1)
                dve.wait_ge(cv_t0, after(e))
                dve.scalar_tensor_tensor(cv_t[:], cv_v[:, 1:T + 1], tap(1), cv_t[:], ALU.mult, ALU.add)\
                   .then_inc(cv_t1, 1)
                dve.wait_ge(cv_t1, after(e))
                dve.scalar_tensor_tensor(cv_t[:], cv_v[:, 0:T], tap(0), cv_t[:], ALU.mult, ALU.add)\
                   .then_inc(cv_t2, 1)
                dve.wait_ge(act_evac, after(4 * e + 3))
                dve.wait_ge(cv_t2, after(e))
                dve.tensor_tensor(cv_b[:], cv_b[:], cv_t[:], ALU.mult).then_inc(cv_t2b, 1)
                dve.wait_ge(cv_t2b, after(e))
                dve.tensor_tensor(cv_t[:], cv_b[:], cv_z[:], ALU.mult).then_inc(y_full, 1)
                dve.wait_ge(y_hi_done, after(e))
                dve.tensor_tensor(y_lo[:, ds(e, 1), :].rearrange("p a t -> p (a t)"), cv_t[:],
                                  y_hi[:, ds(e, 1), :].rearrange("p a t -> p (a t)").bitcast(F32),
                                  ALU.subtract).then_inc(y_lo_done, 1)
                dve.wait_ge(s_ada, 16 * e + 16)
                c = cact[:, ds(e - half * KD, 1)]
                if first:
                    if half == 1:
                        modulation(0)
                    dve.tensor_scalar(adaacc[:], adaw[:], c, None, ALU.mult).then_inc(ada_mac, 1)
                else:
                    dve.wait_ge(ada_mac, after(e - 1))
                    dve.scalar_tensor_tensor(adaacc[:], adaw[:], c, adaacc[:], ALU.mult, ALU.add)\
                       .then_inc(ada_mac, 1)

            for half in range(2):
                conv_chunk(half * KD, half, True)
                with dve.Fori(half * KD + 1, (half + 1) * KD) as e:
                    conv_chunk(e, half, False)
            modulation(1)
            updates(0, onec, B_CONV_OUT + 14, CONV_OUT)

            norm(1, colt[:, C_NORM + KD:C_NORM + 2 * KD], zcol)
            for g in range(G):
                c = C_GAIN + 2 * g
                dve.tensor_scalar(gaint[:, 2 * g:2 * g + 1], colt[:, c:c + 1], HD ** -0.5, None, ALU.mult)
                e = dve.tensor_copy(gaint[:, 2 * g + 1:2 * g + 2], colt[:, c + 1:c + 2])
            e.then_inc(gains, 1)
            dve.wait_ge(gains, after(0))
            dve.wait_ge(s_sel, 16)
            dve.tensor_copy(selr[:], selt[:]).then_inc(gains, 1)

            def squares_split(u, c):
                n = 4 * u + c
                dve.wait_ge(qk_sq, after(n))
                dve.wait_ge(qk_stat, after(u - 1))
                dve.tensor_copy(qksq_hi[:, c, :], nrmb[:, c, :]).then_inc(qksq_hi_done, 1)
                dve.wait_ge(qksq_hi_done, after(n))
                dve.tensor_tensor(qksq_lo[:, c, :], nrmb[:, c, :], qksq_hi[:, c, :].bitcast(F32),
                                  ALU.subtract).then_inc(qksq_lo_done, 1)

            def qk_normalise(u, g):
                dve.wait_ge(s_qkb, 32 * u + 32)
                dve.wait_ge(sc_mm, after(4 * (u - 1) + 3))
                for c in (0, 2, 1, 3):
                    dve.scalar_tensor_tensor(qkn[:, c, :], qkraw[:, c, :],
                                             gaint[:, 2 * g + c // 2:2 * g + c // 2 + 1], nrmb[:, c, :],
                                             ALU.mult, ALU.mult).then_inc(qk_norm, 1)

            def logits(u, g, h):
                if h == 0:
                    dve.wait_ge(s_bias, 16 * u + 16)
                    dve.wait_ge(tr_mm, after(2 * u - 2))
                dve.wait_ge(sc_mm, after(4 * u + h))
                dve.wait_ge(pt_mm, after(4 * u + h - 1))
                if g == 0:
                    dve.tensor_tensor(prob[:, 0:P], psum[:, 2, 0:P], biast[:, h, P:], ALU.add)
                    dve.tensor_tensor(prob[:, P:3 * P], psum[:, 2, P:3 * P], biast[:, h, :], ALU.add)
                    dve.tensor_tensor(prob[:, 3 * P:].rearrange("p (a n) -> p a n", a=2),
                                      psum[:, 3, :].rearrange("p (a n) -> p a n", a=2),
                                      biast[:, h:h + 1, :].broadcast_to([P, 2, 2 * P]), ALU.add)\
                       .then_inc(sc_add, 1)
                    dve.wait_ge(sc_add, after(4 * u + h))
                    dve.tensor_reduce(nmc[:, 0:1, h], prob[:, 0:P], AXX, ALU.max, negate=True)
                    dve.tensor_reduce(nmc[:, 1:4, h], prob[:, P:].rearrange("p (a n) -> p a n", a=3), AXX,
                                      ALU.max, negate=True).then_inc(sc_max, 1)
                else:
                    dve.tensor_tensor(prob[:, 0:4 * P].rearrange("p (a n) -> p a n", a=4),
                                      psum[:, 2, :].rearrange("p (a n) -> p a n", a=4),
                                      biast[:, h:h + 1, 0:P].broadcast_to([P, 4, P]), ALU.add)\
                       .then_inc(sc_add, 1)
                    dve.wait_ge(sc_add, after(4 * u + h))
                    dve.tensor_reduce(nmc[:, :, h], prob[:, 0:4 * P].rearrange("p (a n) -> p a n", a=4), AXX,
                                      ALU.max, negate=True).then_inc(sc_max, 1)

            def turned(u, g, h):
                dve.wait_ge(pt_mm, after(4 * u + h))
                dve.wait_ge(pv_mm, after(4 * u + h - 1))
                if g == 0:
                    dve.tensor_copy(probT[:, 0:4 * P], psum[:, 4, :])
                    dve.tensor_copy(probT[:, 4 * P:], psum[:, 5, 0:3 * P]).then_inc(pt_cp, 1)
                else:
                    dve.tensor_copy(probT[:, 0:4 * P], psum[:, 4, :]).then_inc(pt_cp, 1)

            def natural(ap, g):
                return ap if g == 0 else ap.rearrange("p (i r) -> p r i", r=4)

            def as_queries(ap, g):
                return ap if g == 0 else ap.rearrange("p (r i) -> p r i", r=4)

            def outputs(u, g, c):
                dve.wait_ge(pv_mm, after(4 * u + 2 * c + 1))
                dve.tensor_copy(natural(oacc[:, g, c, :], g), as_queries(psum[:, O, :], g)).then_inc(o_cp, 1)

            def stats(u, g):
                dve.wait_ge(tr_mm, after(2 * u))
                dve.tensor_copy(natural(nrow[:, g, :], g), as_queries(psum[0:HG, ROW, :], g)).then_inc(tr_cp, 1)
                dve.wait_ge(tr_mm, after(2 * u + 1))
                dve.tensor_copy(natural(drow[:, g, :], g), as_queries(psum[0:HG, 4, :], g)).then_inc(tr_cp, 1)

            def qk_reciprocal(u):
                dve.wait_ge(qk_sd, after(u))
                dve.reciprocal(srow[:], srow[:]).then_inc(qk_rstd, 1)

            def merge_max(quad):
                k = 5 * quad
                dve.wait_ge(tr_cp, after(6 * quad + 5))
                dve.tensor_tensor(mrow[:], nrow[:, 0, :], nrow[:, 1, :], ALU.min).then_inc(mg_chain, 1)
                dve.wait_ge(mg_chain, after(k))
                dve.tensor_tensor(mrow[:], mrow[:], nrow[:, 2, :], ALU.min).then_inc(mg_chain, 1)
                dve.wait_ge(mg_chain, after(k + 1))
                dve.tensor_tensor(nrow[:], mrow[:].rearrange("p (a t) -> p a t", a=1).broadcast_to([HG, G, T]),
                                  nrow[:], ALU.subtract).then_inc(mg_max, 1)

            def merge_weights(quad):
                k = 5 * quad
                dve.wait_ge(mg_exp, after(quad))
                dve.tensor_tensor(drow[:], drow[:], nrow[:], ALU.mult).then_inc(mg_chain, 1)
                dve.wait_ge(mg_chain, after(k + 2))
                dve.tensor_tensor(mrow[:], drow[:, 0, :], drow[:, 1, :], ALU.add).then_inc(mg_chain, 1)
                dve.wait_ge(mg_chain, after(k + 3))
                dve.tensor_tensor(mrow[:], mrow[:], drow[:, 2, :], ALU.add).then_inc(mg_chain, 1)
                dve.wait_ge(mg_chain, after(k + 4))
                dve.reciprocal(mrow[:], mrow[:]).then_inc(mg_f, 1)

            def weighed_sum(quad, c, f=fb):
                k = 5 * (2 * quad + c)
                if f is fb1:
                    dve.wait_ge(s_fb1, 32)
                else:
                    dve.wait_ge(s_fb, 32 * (2 * quad + c) + 32)
                total = oacc[:, 0, c, :]
                dve.tensor_tensor(total, total, f[:, 0:T], ALU.mult).then_inc(ym_chain, 1)
                for g in (1, 2):
                    dve.wait_ge(ym_chain, after(k + 2 * g - 3))
                    dve.tensor_tensor(yu[:], oacc[:, g, c, :], f[:, g * T:(g + 1) * T], ALU.mult)\
                       .then_inc(ym_chain, 1)
                    dve.wait_ge(ym_chain, after(k + 2 * g - 1))
                    dve.tensor_tensor(total, total, yu[:], ALU.add).then_inc(ym_chain, 1)
                    dve.wait_ge(ym_chain, after(k + 2 * g))

            def merged(quad, c, f=fb):
                y = Y_ATT + 2 * quad + c
                if f is fb1:
                    dve.wait_ge(s_fsb1, 32)
                else:
                    dve.wait_ge(s_fsb, 32 * (2 * quad + c) + 32)
                dve.wait_ge(y_lo_done, after(y - 1))
                dve.tensor_tensor(yt[:], zs[:, c, :], f[:, G * T:(G + 1) * T], ALU.mult).then_inc(ym_gate, 1)
                dve.wait_ge(ym_gate, after(2 * quad + c))
                dve.tensor_tensor(yt[:], oacc[:, 0, c, :], yt[:], ALU.mult).then_inc(y_full, 1)
                dve.wait_ge(y_full, after(y))
                at = ds(2 * quad + c, 1)
                dve.tensor_copy(ya_hi[:, at, :].rearrange("p a t -> p (a t)"), yt[:]).then_inc(y_hi_done, 1)
                dve.wait_ge(y_hi_done, after(y))
                dve.tensor_tensor(ya_lo[:, at, :].rearrange("p a t -> p (a t)"), yt[:],
                                  ya_hi[:, at, :].rearrange("p a t -> p (a t)").bitcast(F32), ALU.subtract)\
                   .then_inc(y_lo_done, 1)

            def att_unit(quad, g, merge):
                p, pg, u = 3 * quad + g - 1, g - 1, 3 * quad + g
                qk_normalise(p, pg)
                logits(p, pg, 0)
                squares_split(u, 0)
                logits(p, pg, 1)
                turned(p, pg, 0)
                squares_split(u, 1)
                logits(p, pg, 2)
                turned(p, pg, 1)
                squares_split(u, 2)
                if merge:
                    weighed_sum(quad - 1, 0)
                    merged(quad - 1, 0)
                logits(p, pg, 3)
                turned(p, pg, 2)
                squares_split(u, 3)
                outputs(p, pg, 0)
                turned(p, pg, 3)
                qk_reciprocal(u)
                if merge:
                    weighed_sum(quad - 1, 1)
                    merged(quad - 1, 1)
                outputs(p, pg, 1)
                stats(p, pg)

            def att_last(quad, more):
                p = 3 * quad + 2
                qk_normalise(p, 2)
                logits(p, 2, 0)
                logits(p, 2, 1)
                turned(p, 2, 0)
                logits(p, 2, 2)
                turned(p, 2, 1)
                if more:
                    squares_split(p + 1, 0)
                logits(p, 2, 3)
                turned(p, 2, 2)
                if more:
                    squares_split(p + 1, 1)
                outputs(p, 2, 0)
                turned(p, 2, 3)
                if more:
                    squares_split(p + 1, 2)
                outputs(p, 2, 1)
                stats(p, 2)
                if more:
                    squares_split(p + 1, 3)
                merge_max(quad)
                if more:
                    qk_reciprocal(p + 1)
                merge_weights(quad)

            dve.wait_ge(s_xsave, 16)
            for c in range(4):
                squares_split(0, c)
            qk_reciprocal(0)
            att_unit(0, 1, False)
            with dve.Fori(0, NQUAD - 1) as quad:
                att_unit(quad, 2, False)
                att_last(quad, True)
                att_unit(quad + 1, 1, True)
            att_unit(NQUAD - 1, 2, False)
            att_last(NQUAD - 1, False)
            weighed_sum(NQUAD - 1, 0)
            weighed_sum(NQUAD - 1, 1, fb1)
            merged(NQUAD - 1, 0)
            merged(NQUAD - 1, 1, fb1)

            dve.memset(pad[:, :, 0:KC2 - 1], 0.0)
            dve.wait_ge(s_xback, 16)
            updates(1, onec, B_ATT_OUT + 6, ATT_OUT)
            dve.wait_ge(s_lc, 32)

            def layer(l):
                n0, v0, u0 = B_LAYER + LAYER_B * l, V_LAYER + V_PER * l, NCELL * l
                dve.wait_ge(x_upd, after(KD * (2 + l) - 1))
                dve.tensor_copy(lmod[:], mods[:, ds(l, 1), :].rearrange("p a n -> p (a n)")).then_inc(l_mod, 1)
                dve.wait_ge(l_mod, after(l))
                norm(2 + l, lmod[:, KD:2 * KD], lmod)

                d0 = G_DVE * l

                def gate(i, instruction):
                    instruction.then_inc(g_dve, 1)
                    dve.wait_ge(g_dve, after(d0 + i))

                def gate_rows():
                    dve.memset(rstd[0:CH, :], 1.0)
                    dve.wait_ge(g_act, after(G_ACT * l + 2))
                    gate(0, dve.tensor_scalar(g_f, g_f, 0.0, None, ALU.min))
                    gate(1, dve.tensor_tensor(g_f, g_f, g_b, ALU.subtract))
                    gate(2, dve.tensor_tensor_scan(g_b, rstd[0:CH, :], g_f, 0.0, ALU.mult, ALU.add))
                    gate(3, dve.tensor_tensor(g_c, g_i, g_b, ALU.subtract))
                    gate(4, dve.tensor_tensor_scan(g_max, g_c, g_c, 0.0, ALU.max, ALU.max))
                    gate(5, dve.tensor_tensor(g_m, g_b, g_max, ALU.add))
                    gate(6, dve.tensor_scalar(g_f, g_max, -1.0, None, ALU.mult))

                def add_tiles(U):
                    dve.wait_ge(hc_done, after(U))
                    dve.tensor_tensor(sq[:, 0, :], hc[:, 0, :], hc[:, 1, :], ALU.add).then_inc(h_sum, 1)

                def centre(U):
                    for c in range(2):
                        dve.wait_ge(mean_mm, after(U))
                        dve.scalar_tensor_tensor(hc[:, c, :], psum[:, AUX, :], -1.0 / HC, hc[:, c, :], ALU.mult,
                                                 ALU.add).then_inc(cen, 1)
                    dve.wait_ge(c_sq, after(2 * U + 1))
                    dve.tensor_tensor(sq[:, 0, :], sq[:, 0, :], sq[:, 1, :], ALU.add).then_inc(sq_sum, 1)

                def v_low(U, i):
                    for b in range(2):
                        dve.wait_ge(act_evac, after(v0 + i + b))
                        hi = v_hi[:, 2 * b:2 * b + 2, :].rearrange("p a n -> p (a n)")
                        dve.tensor_tensor(v_lo[:, 2 * b:2 * b + 2, :].rearrange("p a n -> p (a n)"),
                                          psum[:, b, :], hi.bitcast(F32), ALU.subtract).then_inc(v_free, 1)

                def finish(U, yb, at, mlstm, v_unit=None, v_block=None):
                    dve.wait_ge(c_sd, after(U))
                    dve.reciprocal(rstd[:], rstd[:]).then_inc(c_rstd, 1)
                    if v_unit is not None:
                        v_low(v_unit, v_block)
                    dve.wait_ge(c_rstd, after(U))
                    dve.wait_ge(s_gcol, 16 * U + 16)
                    for c in range(2):
                        dve.scalar_tensor_tensor(hc[:, c, :], hc[:, c, :], gcol[:, c:c + 1], rstd[:],
                                                 ALU.mult, ALU.mult).then_inc(n_gain, 1)
                    if mlstm is not None:
                        for c in range(2):
                            dve.wait_ge(n_gain, after(2 * U + c))
                            dve.tensor_tensor(hc[:, c, :], hc[:, c, :], ol[:, c, :], ALU.mult).then_inc(n_o, 1)
                    for c in range(2):
                        if mlstm is not None:
                            dve.wait_ge(n_o, after(2 * mlstm + c))
                        else:
                            dve.wait_ge(n_gain, after(2 * U + c))
                        dve.tensor_tensor(hc[:, c, :], hc[:, c, :], zl[:, c, :], ALU.mult).then_inc(y_full, 1)
                    for c in range(2):
                        dve.wait_ge(y_hi_done, after(yb + c))
                        dst = ds(at + c, 1)
                        dve.tensor_tensor(yl_lo[:, dst, :].rearrange("p a t -> p (a t)"), hc[:, c, :],
                                          yl_hi[:, dst, :].rearrange("p a t -> p (a t)").bitcast(F32),
                                          ALU.subtract).then_inc(y_lo_done, 1)

                def weights_low(U, pieces):
                    for i in pieces:
                        _, w0, w1 = S_PIECES[i]
                        dve.wait_ge(wgt_hi_done, after(NP * U + i))
                        dve.tensor_tensor(wgt_lo[:, w0:w1], wgt[:, w0:w1], wgt_hi[:, w0:w1].bitcast(F32),
                                          ALU.subtract).then_inc(wgt_lo_done, 1)

                def decayed(U, h):
                    dve.wait_ge(st_mm, after(U))
                    dve.wait_ge(nv_mm, after(U - 1))
                    for st in range(4):
                        bank, col, w0 = S_AT[st]
                        width = T - st * P
                        e = dve.tensor_tensor(wgt[:, w0:w0 + width], psum[:, bank, col:col + width],
                                              dect[:, ds(h, 1), 0:width].rearrange("p a t -> p (a t)"), ALU.mult)
                        if st != 2:
                            e.then_inc(a_done, 1)
                    weights_low(U, range(NP))

                def weighed(U, H):
                    dve.wait_ge(st_mm, after(U))
                    dve.wait_ge(w_exp, after(H))
                    for bank, w0, w1 in S_PIECES:
                        dve.scalar_tensor_tensor(wgt[:, w0:w1], psum[:, bank, 0:w1 - w0], HC ** -0.5,
                                                 wgt[:, w0:w1], ALU.mult, ALU.mult).then_inc(a_done, 1)
                    k = 3 * H
                    dve.wait_ge(a_done, after(NP * U + NP - 1))
                    dve.tensor_copy(nmb[:, 0:P], wgt[:, 0:P])
                    dve.tensor_tensor(nmb[:, P:], wgt[:, P:T], wgt[:, T:T + 3 * P], ALU.add).then_inc(w_sum_t, 1)
                    dve.wait_ge(w_sum_t, after(k))
                    w2, w3 = S_AT[2][2], S_AT[3][2]
                    dve.tensor_tensor(nmb[:, 2 * P:], nmb[:, 2 * P:], wgt[:, w2:w2 + 2 * P], ALU.add)\
                       .then_inc(w_sum_t, 1)
                    dve.wait_ge(w_sum_t, after(k + 1))
                    dve.tensor_tensor(nmb[:, 3 * P:], nmb[:, 3 * P:], wgt[:, w3:w3 + P], ALU.add)\
                       .then_inc(w_sum_t, 1)
                    dve.wait_ge(w_sum_t, after(k + 2))
                    dve.nop().then_inc(w_sum, 1)
                    weights_low(U, range(NP))

                def qk_low(U, c):
                    dve.wait_ge(qk_hi_done, after(4 * U + c))
                    dve.wait_ge(nv_mm, after(U - 1))
                    dve.tensor_tensor(qk_lo[:, c, :], tmp[:, c % 2, :], qk_hi[:, c, :].bitcast(F32),
                                      ALU.subtract).then_inc(qk_lo_done, 1)

                def conv(H, U, c, n):
                    k = 3 * (4 * H + c)
                    src, dst = pad[:, c % 2, :], tmp[:, c % 2, :]
                    w = hcol[:, c * (KC2 + 1):(c + 1) * (KC2 + 1)]
                    dve.wait_ge(act_evac, after(n))
                    dve.wait_ge(qk_lo_done, after(4 * U + c - 2))
                    dve.tensor_scalar(dst, src[:, 3:], w[:, 3:4], w[:, 4:5], ALU.mult, ALU.add).then_inc(cvl_t, 1)
                    for j in range(2):
                        dve.wait_ge(cvl_t, after(k + j))
                        dve.scalar_tensor_tensor(dst, src[:, 2 - j:2 - j + T], w[:, 2 - j:3 - j], dst,
                                                 ALU.mult, ALU.add).then_inc(cvl_t, 1)
                    dve.wait_ge(cvl_t, after(k + 2))
                    dve.scalar_tensor_tensor(dst, src[:, 0:T], w[:, 0:1], dst, ALU.mult, ALU.add)\
                       .then_inc(cvl, 1)

                def rotate(H, i, n, U):
                    a, b = pad[:, 0, KC2 - 1:], pad[:, 1, KC2 - 1:]
                    k = 7 * (2 * H + i)
                    dve.wait_ge(act_evac, after(n))
                    dve.wait_ge(qk_lo_done, after(4 * U + 2 * i - 1))
                    dve.tensor_tensor(tmp[:, 0, :], a, cosb[:], ALU.mult).then_inc(rot_t, 1)
                    dve.tensor_tensor(tmp[:, 1, :], b, sinb[:], ALU.mult).then_inc(rot_t, 1)
                    dve.wait_ge(rot_t, after(k + 1))
                    dve.tensor_tensor(tmp[:, 0, :], tmp[:, 0, :], tmp[:, 1, :], ALU.subtract).then_inc(rot_t, 1)
                    dve.wait_ge(rot_t, after(k + 2))
                    dve.tensor_tensor(tmp[:, 1, :], a, sinb[:], ALU.mult).then_inc(rot_t, 1)
                    dve.tensor_tensor(b, b, cosb[:], ALU.mult).then_inc(rot_t, 1)
                    dve.wait_ge(rot_t, after(k + 4))
                    dve.tensor_tensor(tmp[:, 1, :], b, tmp[:, 1, :], ALU.add).then_inc(rot_t, 1)
                    dve.wait_ge(rot_t, after(k + 5))
                    dve.nop().then_inc(rot_t, 1)
                    dve.nop().then_inc(rot_d, 1)
                    for c in range(2):
                        qk_low(U, 2 * i + c)

                def mlstm(h, i, before):
                    H, U, yb = CH * l + h, u0 + 2 * h, Y_LAYER + KE * l + 4 * h
                    if before:
                        decayed(U - 1, h - 1)
                    dve.wait_ge(s_hcol, 16 * H + 16)
                    first = i if before else 0
                    conv(H, U, 0, v0 + first)
                    if before:
                        dve.wait_ge(nv_mm, after(U - 1))
                        for c in range(2):
                            e = dve.tensor_copy(hc[:, c, :], psum[:, NUM + c, :])
                        e.then_inc(hc_done, 1)
                        add_tiles(U - 1)
                    conv(H, U, 1, v0 + first + 1)
                    if not before:
                        dve.wait_ge(s_xsave, 16 * l + 32)
                    qk_low(U, 0)
                    qk_low(U, 1)
                    if before:
                        centre(U - 1)
                    conv(H, U, 2, v0 + i + 2)
                    if not before:
                        gate_rows()
                    conv(H, U, 3, v0 + i + 3)
                    qk_low(U, 2)
                    qk_low(U, 3)
                    if before:
                        finish(U - 1, yb - 2, KD + 2 * (h - 1), None, U, i + 4)
                    else:
                        v_low(U, i + 4)
                        dve.wait_ge(cc_mm, after(l))
                        dve.tensor_copy(ccol[:].rearrange("p a b -> p (a b)"), psum[:, AUX, 0:4 * CH])\
                           .then_inc(cc_cp, 1)
                    dve.wait_ge(s_crb, 32 * H + 32)
                    dve.wait_ge(w_exp, after(H - 1))
                    dve.wait_ge(cc_cp, after(l))
                    dve.tensor_copy(cch[:], ccol[:, :, ds(h, 1)].rearrange("p a b -> p (a b)"))
                    dve.tensor_tensor(argd[:], nmb[:].rearrange("p (a b) -> p a b", a=4),
                                      trit[:].rearrange("p (a b) -> p a b", a=1).broadcast_to([P, 4, P]),
                                      ALU.add).then_inc(w_arg, 1)

                def retention(h, i):
                    H, U, yb = CH * l + h, u0 + 2 * h + 1, Y_LAYER + KE * l + 4 * h + 2
                    weighed(U - 1, H)
                    dve.wait_ge(den_abs, after(H))
                    dve.tensor_tensor(rstd[:], rstd[:], emb[:], ALU.max).then_inc(den_max, 1)
                    dve.wait_ge(den_max, after(H))
                    dve.reciprocal(rstd[:], rstd[:]).then_inc(den_rec, 1)
                    dve.wait_ge(den_rec, after(H))
                    for c in range(2):
                        e = dve.tensor_tensor(hc[:, c, :], psum[:, NUM + c, :], rstd[:], ALU.mult)
                    e.then_inc(hc_done, 1)
                    add_tiles(U - 1)
                    rotate(H, 0, v0 + i + 1, U)
                    centre(U - 1)
                    rotate(H, 1, v0 + i + 3, U)
                    finish(U - 1, yb - 2, 2 * h, H, U, i + 4)

                mlstm(0, GATE_B, False)
                retention(0, GATE_B + 10)
                with dve.Fori(1, CH) as h:
                    mlstm(h, GATE_B + 18 * h, True)
                    retention(h, GATE_B + 18 * h + 10)
                U = u0 + NCELL - 1
                decayed(U, CH - 1)
                dve.wait_ge(nv_mm, after(U))
                for c in range(2):
                    e = dve.tensor_copy(hc[:, c, :], psum[:, NUM + c, :])
                e.then_inc(hc_done, 1)
                add_tiles(U)
                centre(U)
                finish(U, Y_LAYER + KE * l + KE - 2, KE - 2, None)
                dve.wait_ge(s_xback, 16 * l + 32)
                updates(2 + l, lmod[:, 2 * KD:], n0 + GATE_B + CELL_B + 14, LAYER_OUT)

            with dve.Fori(0, NL) as l:
                layer(l)
            norm_root(4)
            for k in range(KD):
                c = C_NORM + 4 * KD + k
                dve.scalar_tensor_tensor(xs[:, k, :], xs[:, k, :], colt[:, c:c + 1], psum[:, NORM, :],
                                         ALU.mult, ALU.mult).then_inc(h_full, 1)


def chunk(w, c0, k0=0):
    return w[k0 * P:(k0 + KD) * P, c0:c0 + P].reshape(KD, P, P).transpose(1, 0, 2).reshape(P, BLK)


def value_chunks(w, c0):
    return [w[b * 4 * P:(b + 1) * 4 * P, c0:c0 + HC].reshape(4, P, HC).transpose(1, 0, 2).reshape(P, BLK)
            for b in range(2)]


def out_chunks(w):
    def part(pair, group):
        return w[2 * pair * P:2 * (pair + 1) * P, group * 4 * P:(group + 1) * 4 * P]\
            .reshape(2, P, 4, P).transpose(1, 2, 0, 3).reshape(P, BLK)

    last = w.shape[0] // (2 * P) - 1
    return [part(pair, group) for group in range(2) for pair in range(last)] + [part(last, 0), part(last, 1)]


def weight_stream(conv_w_in, conv_w_out, attn_w_in, attn_w_out, w_in_2, w_out_2):
    blocks = [chunk(conv_w_in[0], part * E_CONV + e * P) for e in range(KE) for part in (1, 2, 3, 0)]
    blocks += out_chunks(conv_w_out[0])
    w = attn_w_in[0]
    for quad in range(NQUAD):
        for g in range(G):
            at = lambda part: (g * 3 + part) * D + quad * HG * HD
            blocks += [chunk(w, at(part) + c * P) for part in range(2) for c in range(2)]
            blocks += value_chunks(w, at(2))
        blocks += [chunk(w, 9 * D + quad * HG * HD + c * P) for c in range(2)]
    blocks += out_chunks(attn_w_out[0])
    for l in range(NL):
        w = w_in_2[l]
        gates = np.zeros((D, P), w.dtype)
        gates[:, 0:CH] = w[:, 5 * D:5 * D + CH]
        gates[:, 32:32 + CH] = w[:, 5 * D + CH:5 * D + 2 * CH]
        gate_blocks = []
        for b in range(GATE_B):
            half = np.zeros((P, BLK), w.dtype)
            half[:, 0:4 * P] = gates[b * 4 * P:(b + 1) * 4 * P].reshape(4, P, P).transpose(1, 0, 2).reshape(P, 4 * P)
            gate_blocks.append(half)
        m, r = 0, 5 * D + 2 * CH
        for h in range(CH):
            for part in (0, 1):
                blocks += [chunk(w, m + part * D + h * HC + c * P) for c in range(2)]
                if h == 0 and part == 0:
                    blocks += gate_blocks
            blocks += value_chunks(w, m + 2 * D + h * HC)
            for part in (3, 4):
                blocks += [chunk(w, m + part * D + h * HC + c * P) for c in range(2)]
            for part in (0, 1):
                blocks += [chunk(w, r + part * D + h * HC + c * P) for c in range(2)]
            blocks += value_chunks(w, r + 2 * D + h * HC)
            blocks += [chunk(w, r + 3 * D + h * HC + c * P) for c in range(2)]
        blocks += out_chunks(w_out_2[l])
    return np.stack(blocks)


def by_partition(v):
    return np.ascontiguousarray(v.reshape(-1, P).T)


def bucket(dist):
    exact = NBUCKET // 2
    d = np.maximum(dist, 1).astype(np.float32)
    large = exact + (np.log(d / exact) / math.log(MAXDIST / exact) * (NBUCKET - exact)).astype(np.int32)
    return np.where(dist < exact, dist, np.minimum(large, NBUCKET - 1))


def shape_constants():
    onehot = np.zeros((NBUCKET + 1, NE), np.float32)
    onehot[NBUCKET] = NEG
    for n in range(2 * P + P - 1):
        step = 2 * P - 1 - n
        if 0 <= step <= P:
            onehot[:, n] = 0
            onehot[bucket(np.int32(step * DILATION[0])), n] = 1
    for n in range(P):
        for g in (1, 2):
            if (P - 1 - n) % (DILATION[g] // 4) == 0:
                col = W0 + (g - 1) * W1 + n
                onehot[:, col] = 0
                onehot[bucket(np.int32(4 * (P - 1 - n))), col] = 1
    s, t = np.arange(P)[:, None], np.arange(T)[None]
    gamma = np.log(1.0 - 2.0 ** (-5.0 - np.arange(CH)))
    decay = np.where(t >= s, np.exp(gamma[:, None, None] * np.maximum(t - s, 0)) * HC ** -0.5, 0.0)
    sel = np.zeros((P, 4, 2 * HG), np.float32)
    for c in range(4):
        sel[:HD, c, 2 * c] = sel[HD:, c, 2 * c + 1] = 1
    freq = (np.float32(1) / np.float32(10000.0) ** np.linspace(0, 1, P, dtype=np.float32)).astype(np.float32)
    return {
        "onehot": onehot, "ident": np.eye(P, dtype=np.float32),
        "tri": np.where(s > t[:, :P], NEG, 0).astype(np.float32),
        "decay": np.ascontiguousarray(decay.transpose(1, 0, 2)).astype(np.float32), "sel": sel,
    }, freq[:, None]


def kernel(x, conv_norm, conv_w_in, conv_w, conv_w_out, attn_norm, attn_w_in, attn_q_gain, attn_k_gain,
           attn_w_out, rel_bias, c_2, positions_2, w_ada_2, b_ada_2, norm_g_2, w_in_2, conv_w_2, conv_b_2,
           b_igate_2, b_fgate_2, gn_m_2, gn_r_2, w_out_2, final_g_2):
    import concourse.bacc as bacc
    from concourse.bass_utils import run_bass_kernel_spmd as run

    consts, freq = shape_constants()
    gains = [np.concatenate([v[0, g], v[0, g]])[:, None] for g in range(G) for v in (attn_q_gain, attn_k_gain)]
    cols = np.concatenate(
        [by_partition(conv_norm), by_partition(attn_norm), by_partition(norm_g_2), by_partition(final_g_2),
         by_partition(conv_w), *gains, by_partition(b_ada_2), by_partition(c_2), freq], axis=1)
    taps = np.concatenate([conv_w_2, conv_b_2[:, None]], axis=1).reshape(NL, KC2 + 1, 2, CH, 2, P)
    headcols = taps.transpose(0, 3, 5, 2, 4, 1).reshape(NL * CH, P, 4 * (KC2 + 1))
    gn = np.stack([gn_m_2.reshape(NL, CH, 2, P), gn_r_2.reshape(NL, CH, 2, P)], axis=2)
    gncols = gn.transpose(0, 1, 2, 4, 3).reshape(NL * NCELL, P, 2)
    gatecols = np.zeros((NL, 64, 1), b_igate_2.dtype)
    gatecols[:, 0:CH, 0] = b_igate_2
    gatecols[:, 32:32 + CH, 0] = b_fgate_2
    arrays = {
        "x": x[0].T.reshape(KD, P, T),
        "wstream": weight_stream(conv_w_in, conv_w_out, attn_w_in, attn_w_out, w_in_2, w_out_2),
        "wada": w_ada_2.reshape(NL * KD, P, 3 * D),
        "cols": cols, "headcols": headcols, "gncols": gncols, "gatecols": gatecols, "relb": rel_bias,
        "onehot": consts["onehot"], "pos": positions_2.reshape(1, T), "ident": consts["ident"],
        "tri": consts["tri"], "decay": consts["decay"], "sel": consts["sel"],
    }
    nc = bacc.Bacc("TRN2", target_bir_lowering=False, num_devices=1)
    ins, args = {}, []
    for name, a in arrays.items():
        ins[f"in_{name}"] = a = np.ascontiguousarray(a)
        args.append(nc.dram_tensor(f"in_{name}", a.shape, mybir.dt.from_np(a.dtype), kind="ExternalInput").ap())
    args.append(nc.dram_tensor("out", (KD, P, T), F32, kind="ExternalOutput").ap())
    program(nc, *args)
    r = run(nc, [ins], core_ids=[0])
    return np.ascontiguousarray(r.results[0]["out"].reshape(D, T).T).reshape(1, T, D)
```
